# Optimizing a Trainium2 kernel written in Bass

```python
import jax, jax.numpy as jnp
from jax import lax
import numpy as np
import math
import jax
import jax.numpy as jnp

D_MODEL = 2048
BATCH = 1
SEQ = 512
DEPTH = 2

W_CONV = D_MODEL // 2
HEAD_DIM = 64
N_Q_HEADS = (D_MODEL // 2) // HEAD_DIM
N_KV_HEADS = N_Q_HEADS // 4
GQA_GROUP = N_Q_HEADS // N_KV_HEADS
W_ATT = N_Q_HEADS * HEAD_DIM
W_KV = N_KV_HEADS * HEAD_DIM
W_MIX = W_CONV + W_ATT
IN_SPLITS = [W_CONV, W_CONV, W_CONV, W_ATT, W_KV, W_KV, W_ATT]
W_IN = sum(IN_SPLITS)
CONV_WIDTH = 31
CONV_PAD = CONV_WIDTH // 2
WINDOW = 128
BLK = 128
NUM_BUCKETS = 32
MAX_DISTANCE = 128
PLE_DIM = 256
EPS = 1e-6
NEG = -1e30


def _rmsnorm(x, g):
    xf = x.astype(jnp.float32)
    y = xf * lax.rsqrt(jnp.mean(xf * xf, axis=-1, keepdims=True) + EPS)
    return (y * g.astype(jnp.float32)).astype(x.dtype)

def _layernorm(x, g, b):
    xf = x.astype(jnp.float32)
    mu = jnp.mean(xf, axis=-1, keepdims=True)
    xc = xf - mu
    y = xc * lax.rsqrt(jnp.mean(xc * xc, axis=-1, keepdims=True) + EPS)
    return (y * g.astype(jnp.float32) + b.astype(jnp.float32)).astype(x.dtype)

def _t5_band_buckets():
    q_off = np.arange(BLK)[:, None]
    k_off = np.arange(3 * BLK)[None, :] - BLK
    rel = k_off - q_off
    half = NUM_BUCKETS // 2
    ret = (rel > 0).astype(np.int32) * half
    n = np.abs(rel)
    max_exact = half // 2
    large = max_exact + (np.log(np.maximum(n, 1) / max_exact)
                         / np.log(MAX_DISTANCE / max_exact)
                         * (half - max_exact)).astype(np.int32)
    large = np.minimum(large, half - 1)
    ret = ret + np.where(n < max_exact, n, large)
    return ret.astype(np.int32), (n <= WINDOW)

def _band_bias(rel_bias):
    buckets, band = _t5_band_buckets()
    bias = jnp.take(rel_bias.astype(jnp.float32), jnp.asarray(buckets), axis=0)
    bias = jnp.transpose(bias, (2, 0, 1))
    bias = jnp.where(jnp.asarray(band)[None], bias, NEG)
    return bias.reshape(N_KV_HEADS, GQA_GROUP, BLK, 3 * BLK)

def _window_attention(q, k, v, bias_band, sink):
    B, S = q.shape[0], q.shape[1]
    nb = S // BLK
    scale = HEAD_DIM ** -0.5
    k_pad = jnp.pad(k, ((0, 0), (BLK, BLK), (0, 0), (0, 0)))
    v_pad = jnp.pad(v, ((0, 0), (BLK, BLK), (0, 0), (0, 0)))
    sink_f = sink.astype(jnp.float32).reshape(N_KV_HEADS, GQA_GROUP, 1)
    key_off = jnp.arange(3 * BLK) - BLK

    def one_block(b):
        start = b * BLK
        qb = lax.dynamic_slice_in_dim(q, start, BLK, axis=1)
        kb = lax.dynamic_slice_in_dim(k_pad, start, 3 * BLK, axis=1)
        vb = lax.dynamic_slice_in_dim(v_pad, start, 3 * BLK, axis=1)
        s = jnp.einsum('bqkgd,bskd->bkgqs', qb, kb,
                       preferred_element_type=jnp.float32) * scale + bias_band
        kpos = start + key_off
        valid = (kpos >= 0) & (kpos < S)
        s = jnp.where(valid, s, NEG)
        m = jnp.maximum(jnp.max(s, axis=-1), sink_f)
        e = jnp.exp(s - m[..., None])
        denom = jnp.sum(e, axis=-1) + jnp.exp(sink_f - m)
        pr = (e / denom[..., None]).astype(vb.dtype)
        return jnp.einsum('bkgqs,bskd->bqkgd', pr, vb)

    out = lax.map(one_block, jnp.arange(nb))
    return jnp.moveaxis(out, 0, 1).reshape(B, S, W_ATT)

def _conformer_conv(a_val, a_glu, conv_w, conv_b, cln_g, cln_b):
    a = a_val * jax.nn.sigmoid(a_glu)
    y = lax.conv_general_dilated(
        a, conv_w[:, None, :].astype(a.dtype), window_strides=(1,),
        padding=[(CONV_PAD, CONV_PAD)], dimension_numbers=('NWC', 'WIO', 'NWC'),
        feature_group_count=W_CONV) + conv_b
    y = _layernorm(y, cln_g, cln_b)
    return jax.nn.silu(y)

def first_inputs(seed: int = 0) -> dict:
    key = jax.random.key(seed)
    ks = jax.random.split(key, 16)
    f32 = jnp.float32
    nrm = lambda k, shp, s: (jax.random.normal(k, shp, f32) * s)
    return {
        "x": nrm(ks[0], (BATCH, SEQ, D_MODEL), 1.0),
        "p": nrm(ks[1], (DEPTH, BATCH, SEQ, PLE_DIM), 1.0),
        "norm_g": 1.0 + nrm(ks[2], (DEPTH, D_MODEL), 0.02),
        "w_in": nrm(ks[3], (DEPTH, D_MODEL, W_IN), D_MODEL ** -0.5),
        "conv_w": nrm(ks[4], (DEPTH, CONV_WIDTH, W_CONV), CONV_WIDTH ** -0.5),
        "conv_b": nrm(ks[5], (DEPTH, W_CONV), 0.02),
        "cln_g": 1.0 + nrm(ks[6], (DEPTH, W_CONV), 0.02),
        "cln_b": nrm(ks[7], (DEPTH, W_CONV), 0.02),
        "sink": nrm(ks[8], (DEPTH, N_Q_HEADS), 0.5),
        "rel_bias": nrm(ks[9], (NUM_BUCKETS, N_Q_HEADS), 0.5),
        "w_out": nrm(ks[10], (DEPTH, W_MIX, D_MODEL), W_MIX ** -0.5),
        "w_pe": nrm(ks[11], (DEPTH, PLE_DIM, D_MODEL), PLE_DIM ** -0.5),
        "pe_g": 1.0 + nrm(ks[12], (DEPTH, D_MODEL), 0.02),
        "w_pg": nrm(ks[13], (DEPTH, D_MODEL, D_MODEL), D_MODEL ** -0.5),
        "final_g": 1.0 + nrm(ks[14], (D_MODEL,), 0.02),
    }

def first_block(x, p, norm_g, w_in, conv_w, conv_b, cln_g, cln_b, sink, rel_bias,
              w_out, w_pe, pe_g, w_pg, final_g):
    B, S, _ = x.shape
    bias_band = _band_bias(rel_bias)
    offs = np.cumsum(IN_SPLITS)[:-1].tolist()
    h = x
    for i in range(DEPTH):
        hn = _rmsnorm(h, norm_g[i])
        u = hn @ w_in[i]
        a_val, a_glu, a_z, q, k, v, b_z = jnp.split(u, offs, axis=-1)
        ya = _conformer_conv(a_val, a_glu, conv_w[i], conv_b[i], cln_g[i], cln_b[i])
        ya = ya * jax.nn.silu(a_z)
        q = q.reshape(B, S, N_KV_HEADS, GQA_GROUP, HEAD_DIM)
        k = k.reshape(B, S, N_KV_HEADS, HEAD_DIM)
        v = v.reshape(B, S, N_KV_HEADS, HEAD_DIM)
        yb = _window_attention(q, k, v, bias_band, sink[i]) * jax.nn.silu(b_z)
        h = h + jnp.concatenate([ya, yb], axis=-1) @ w_out[i]
        e = _rmsnorm(p[i] @ w_pe[i], pe_g[i])
        h = h + e * jax.nn.sigmoid(h @ w_pg[i])
    return _rmsnorm(h, final_g)


DEPTH_2 = 1

N_MIXERS = 3
NORM_EPS = 1e-6
NEG_INF = -1e30
TINY = 1e-30
Q_BLOCK = 128

N_BUCKETS = 32
BUCKET_MAX_DIST = 2048
N_BIAS_HEADS = 16

LRU_WIDTH = D_MODEL
LRU_BLOCKS = 8
LRU_BLOCK_W = LRU_WIDTH // LRU_BLOCKS
CONV_W = 4
LRU_C = 8.0

DIL_PATTERNS = ((128, 1), (512, 4), (2048, 16))
N_DIL = len(DIL_PATTERNS)
DIL_HEADS = 16
DIL_HEAD_DIM = 64
DIL_WIDTH = DIL_HEADS * DIL_HEAD_DIM
DIL_IN_COLS = N_DIL * 3 * DIL_WIDTH + DIL_WIDTH

NSA_HEADS = 16
NSA_KV_GROUPS = 4
NSA_REP = NSA_HEADS // NSA_KV_GROUPS
NSA_HEAD_DIM = 128
NSA_WIDTH = NSA_HEADS * NSA_HEAD_DIM
NSA_KV_WIDTH = NSA_KV_GROUPS * NSA_HEAD_DIM
CMP_BLOCK = 32
CMP_STRIDE = 16
CMP_HIDDEN = 512
SEL_BLOCK = 64
SEL_TOPK = 16
WIN = 512
SEL_QCHUNK = 16
FORCE_BONUS = 1e4
NSA_SPLITS = (NSA_WIDTH,) + (NSA_KV_WIDTH,) * 6 + (3 * NSA_HEADS, NSA_WIDTH)
NSA_IN_COLS = sum(NSA_SPLITS)


def _rmsnorm_2(x, g):
    xf = x.astype(jnp.float32)
    y = xf * lax.rsqrt(jnp.mean(xf * xf, axis=-1, keepdims=True) + NORM_EPS)
    return (y * g.astype(jnp.float32)).astype(x.dtype)

def _t5_bucket(dist):
    n = jnp.maximum(dist, 0)
    max_exact = N_BUCKETS // 2
    nf = jnp.maximum(n, max_exact).astype(jnp.float32)
    large = max_exact + (jnp.log(nf / max_exact) / math.log(BUCKET_MAX_DIST / max_exact)
                         * (N_BUCKETS - max_exact)).astype(jnp.int32)
    return jnp.where(n < max_exact, n, jnp.minimum(large, N_BUCKETS - 1))

def _masked_softmax(logits, mask):
    l = jnp.where(mask, logits, NEG_INF)
    m = jnp.max(l, axis=-1, keepdims=True)
    e = jnp.where(mask, jnp.exp(l - m), 0.0)
    s = jnp.sum(e, axis=-1, keepdims=True)
    return e / jnp.maximum(s, TINY), m[..., 0], s[..., 0]

def _unblock(t, length):
    nb, n, qb = t.shape[:3]
    t = jnp.moveaxis(t, 0, 1).reshape((n, nb * qb) + t.shape[3:])
    return t[:, :length]

def _banded_attention(q, k, v, rel_bias, lookback, max_delta, dilation):
    n, length, G, R, dh = q.shape
    nb = -(-length // Q_BLOCK)
    lp = nb * Q_BLOCK
    qp = jnp.pad(q, ((0, 0), (0, lp - length), (0, 0), (0, 0), (0, 0)))
    kp = jnp.pad(k, ((0, 0), (lookback, lp - length), (0, 0), (0, 0)))
    vp = jnp.pad(v, ((0, 0), (lookback, lp - length), (0, 0), (0, 0)))
    table = rel_bias.reshape(N_BUCKETS, G, R)
    span = Q_BLOCK + lookback
    scale = dh ** -0.5

    def block(b):
        q0 = b * Q_BLOCK
        qs = lax.dynamic_slice_in_dim(qp, q0, Q_BLOCK, axis=1)
        ks = lax.dynamic_slice_in_dim(kp, q0, span, axis=1)
        vs = lax.dynamic_slice_in_dim(vp, q0, span, axis=1)
        qpos = q0 + jnp.arange(Q_BLOCK)
        kpos = q0 - lookback + jnp.arange(span)
        delta = qpos[:, None] - kpos[None, :]
        mask = (delta >= 0) & (delta <= max_delta) & (kpos[None, :] >= 0)
        bias = jnp.transpose(table[_t5_bucket(delta * dilation)], (2, 3, 0, 1)).astype(jnp.float32)
        logits = jnp.einsum('nqgrd,nkgd->ngrqk', qs, ks).astype(jnp.float32) * scale + bias
        prob, m, s = _masked_softmax(logits, mask)
        o = jnp.einsum('ngrqk,nkgd->nqgrd', prob, vs.astype(jnp.float32))
        return o, jnp.transpose(m, (0, 3, 1, 2)), jnp.transpose(s, (0, 3, 1, 2))

    o, m, s = lax.map(block, jnp.arange(nb))
    return _unblock(o, length), _unblock(m, length), _unblock(s, length)

def _to_strided(t, d):
    bn, s = t.shape[:2]
    rest = t.shape[2:]
    t = jnp.swapaxes(t.reshape((bn, s // d, d) + rest), 1, 2)
    return t.reshape((bn * d, s // d) + rest)

def _from_strided(t, d, bn):
    n, length = t.shape[:2]
    rest = t.shape[2:]
    t = jnp.swapaxes(t.reshape((bn, d, length) + rest), 1, 2)
    return t.reshape((bn, length * d) + rest)

def _rglru_mixer(u, w_in, conv_w, conv_b, w_r, b_r, w_i, b_i, lam, w_out):
    bn, s, _ = u.shape
    proj = u @ w_in
    xb, gate = proj[..., :LRU_WIDTH], proj[..., LRU_WIDTH:]
    xc = lax.conv_general_dilated(xb, conv_w[:, None, :], window_strides=(1,),
                                  padding=((CONV_W - 1, 0),),
                                  dimension_numbers=('NWC', 'WIO', 'NWC'),
                                  feature_group_count=LRU_WIDTH) + conv_b
    xblk = xc.reshape(bn, s, LRU_BLOCKS, LRU_BLOCK_W)
    r = jax.nn.sigmoid(jnp.einsum('bsnc,ncd->bsnd', xblk, w_r) + b_r).reshape(bn, s, LRU_WIDTH)
    i = jax.nn.sigmoid(jnp.einsum('bsnc,ncd->bsnd', xblk, w_i) + b_i).reshape(bn, s, LRU_WIDTH)
    log_a = -LRU_C * r.astype(jnp.float32) * jax.nn.softplus(-lam.astype(jnp.float32))
    a = jnp.exp(log_a)
    bterm = jnp.sqrt(-jnp.expm1(2.0 * log_a)) * (i * xc).astype(jnp.float32)

    def combine(e1, e2):
        a1, b1 = e1
        a2, b2 = e2
        return a1 * a2, a2 * b1 + b2

    _, h = lax.associative_scan(combine, (a, bterm), axis=1)
    y = h.astype(u.dtype) * jax.nn.silu(gate)
    return y @ w_out

def _dilated_mixer(u, w_in, w_out, rel_bias):
    bn, s, _ = u.shape
    proj = u @ w_in
    qkv = proj[..., :N_DIL * 3 * DIL_WIDTH].reshape(bn, s, N_DIL, 3, DIL_HEADS, 1, DIL_HEAD_DIM)
    gate = proj[..., N_DIL * 3 * DIL_WIDTH:]
    outs, maxes, dens = [], [], []
    for gi, (window, dil) in enumerate(DIL_PATTERNS):
        q = _to_strided(qkv[:, :, gi, 0], dil)
        k = _to_strided(qkv[:, :, gi, 1, :, 0], dil)
        v = _to_strided(qkv[:, :, gi, 2, :, 0], dil)
        o, m, den = _banded_attention(q, k, v, rel_bias, window // dil, window // dil, dil)
        outs.append(_from_strided(o[:, :, :, 0], dil, bn))
        maxes.append(_from_strided(m[:, :, :, 0], dil, bn))
        dens.append(_from_strided(den[:, :, :, 0], dil, bn))
    o = jnp.stack(outs)
    m = jnp.stack(maxes)
    den = jnp.stack(dens)
    wts = den * jnp.exp(m - jnp.max(m, axis=0, keepdims=True))
    o = jnp.sum(wts[..., None] * o, axis=0) / jnp.sum(wts, axis=0)[..., None]
    y = o.reshape(bn, s, DIL_WIDTH).astype(u.dtype) * jax.nn.silu(gate)
    return y @ w_out

def _compress(t, cidx, pos, w1, w2):
    bn, nc = t.shape[0], cidx.shape[0]
    blk = t[:, cidx] + pos[None, None, :, None, :]
    blk = jnp.swapaxes(blk, 2, 3).reshape(bn, nc, NSA_KV_GROUPS, CMP_BLOCK * NSA_HEAD_DIM)
    return jax.nn.gelu(blk @ w1) @ w2

def _nsa_mixer(u, w_in, pos_k, w1_k, w2_k, pos_v, w1_v, w2_v, w_out, rel_bias):
    bn, s, _ = u.shape
    G, R, dh = NSA_KV_GROUPS, NSA_REP, NSA_HEAD_DIM
    scale = dh ** -0.5
    proj = u @ w_in
    offs = np.cumsum(NSA_SPLITS)[:-1].tolist()
    q, kc, vc, ksl, vsl, kw, vw, bgate, gpath = jnp.split(proj, offs, axis=-1)
    q = q.reshape(bn, s, G, R, dh)
    kc, vc, ksl, vsl, kw, vw = [t.reshape(bn, s, G, dh) for t in (kc, vc, ksl, vsl, kw, vw)]

    nc = (s - CMP_BLOCK) // CMP_STRIDE + 1
    cidx = np.arange(nc)[:, None] * CMP_STRIDE + np.arange(CMP_BLOCK)[None, :]
    cend = cidx[:, -1]
    kcmp = _compress(kc, cidx, pos_k, w1_k, w2_k)
    vcmp = _compress(vc, cidx, pos_v, w1_v, w2_v)
    nsel = s // SEL_BLOCK
    topk = min(SEL_TOPK, nsel)
    sel_start = np.arange(nsel) * SEL_BLOCK
    cover = jnp.asarray(((cidx[:, :1] < sel_start[None, :] + SEL_BLOCK)
                         & (cidx[:, -1:] >= sel_start[None, :])).astype(np.float32))
    blk_ids = jnp.arange(nsel)

    def cmp_block(b):
        q0 = b * Q_BLOCK
        qs = lax.dynamic_slice_in_dim(q, q0, Q_BLOCK, axis=1)
        t = q0 + jnp.arange(Q_BLOCK)
        mask = cend[None, :] <= t[:, None]
        logits = jnp.einsum('bqgrd,bcgd->bgrqc', qs, kcmp).astype(jnp.float32) * scale
        prob, _, _ = _masked_softmax(logits, mask)
        o = jnp.einsum('bgrqc,bcgd->bqgrd', prob, vcmp.astype(jnp.float32))
        imp = jnp.einsum('bgrqc,cn->bgqn', prob, cover)
        cur = t // SEL_BLOCK
        forced = ((blk_ids[None, :] == 0) | (blk_ids[None, :] == cur[:, None])
                  | (blk_ids[None, :] == cur[:, None] - 1)).astype(jnp.float32)
        valid = blk_ids[None, :] * SEL_BLOCK <= t[:, None]
        imp = jnp.where(valid, imp + FORCE_BONUS * forced, NEG_INF)
        _, idx = lax.top_k(imp, topk)
        return o, jnp.transpose(idx, (0, 2, 1, 3))

    o_cmp, sel_idx = lax.map(cmp_block, jnp.arange(s // Q_BLOCK))
    o_cmp = _unblock(o_cmp, s)
    sel_idx = _unblock(sel_idx, s)

    ksT = jnp.swapaxes(ksl, 1, 2)
    vsT = jnp.swapaxes(vsl, 1, 2)
    nkeys = topk * SEL_BLOCK
    tgr = jnp.transpose(rel_bias.reshape(N_BUCKETS, G, R), (1, 2, 0))
    g_ix = jnp.arange(G)[None, :, None, None, None]
    r_ix = jnp.arange(R)[None, None, :, None, None]
    gather = jax.vmap(jax.vmap(lambda a, ix: a[ix]))

    def sel_chunk(c):
        q0 = c * SEL_QCHUNK
        qs = lax.dynamic_slice_in_dim(q, q0, SEL_QCHUNK, axis=1)
        idx = lax.dynamic_slice_in_dim(sel_idx, q0, SEL_QCHUNK, axis=1)
        tok = idx[..., None] * SEL_BLOCK + jnp.arange(SEL_BLOCK)
        tok = jnp.transpose(tok.reshape(bn, SEL_QCHUNK, G, nkeys), (0, 2, 1, 3))
        flat = tok.reshape(bn, G, SEL_QCHUNK * nkeys)
        kg = gather(ksT, flat).reshape(bn, G, SEL_QCHUNK, nkeys, dh)
        vg = gather(vsT, flat).reshape(bn, G, SEL_QCHUNK, nkeys, dh)
        t = q0 + jnp.arange(SEL_QCHUNK)
        delta = t[None, None, :, None] - tok
        bias = tgr[g_ix, r_ix, _t5_bucket(delta)[:, :, None]].astype(jnp.float32)
        logits = jnp.einsum('bqgrd,bgqnd->bgrqn', qs, kg).astype(jnp.float32) * scale + bias
        prob, _, _ = _masked_softmax(logits, (delta >= 0)[:, :, None])
        return jnp.einsum('bgrqn,bgqnd->bqgrd', prob, vg.astype(jnp.float32))

    o_sel = _unblock(lax.map(sel_chunk, jnp.arange(s // SEL_QCHUNK)), s)

    o_win, _, _ = _banded_attention(q, kw, vw, rel_bias, WIN, WIN - 1, 1)

    gts = jax.nn.sigmoid(bgate.reshape(bn, s, G, R, 3).astype(jnp.float32))
    o = gts[..., 0:1] * o_cmp + gts[..., 1:2] * o_sel + gts[..., 2:3] * o_win
    y = o.reshape(bn, s, NSA_WIDTH).astype(u.dtype) * jax.nn.silu(gpath)
    return y @ w_out

def second_inputs(seed: int = 0) -> dict:
    key = jax.random.key(seed)
    ks = iter(jax.random.split(key, 40))
    n_a = len(range(0, DEPTH_2, N_MIXERS))
    n_b = len(range(1, DEPTH_2, N_MIXERS))
    n_c = len(range(2, DEPTH_2, N_MIXERS))

    def nrm(shape, scale):
        return scale * jax.random.normal(next(ks), shape, jnp.float32)

    a_dec = jax.random.uniform(next(ks), (n_a, LRU_WIDTH), jnp.float32, minval=0.9, maxval=0.999)
    return {
        "x": nrm((BATCH, SEQ, D_MODEL), 1.0),
        "p": nrm((DEPTH_2, BATCH, SEQ, PLE_DIM), 1.0),
        "rel_bias": nrm((N_BUCKETS, N_BIAS_HEADS), 0.5),
        "norm_pre": 1.0 + nrm((DEPTH_2, D_MODEL), 0.05),
        "norm_post": 1.0 + nrm((DEPTH_2, D_MODEL), 0.05),
        "ple_w_proj": nrm((DEPTH_2, PLE_DIM, D_MODEL), PLE_DIM ** -0.5),
        "ple_w_gate": nrm((DEPTH_2, D_MODEL, D_MODEL), D_MODEL ** -0.5),
        "a_w_in": nrm((n_a, D_MODEL, 2 * LRU_WIDTH), D_MODEL ** -0.5),
        "a_conv_w": nrm((n_a, CONV_W, LRU_WIDTH), CONV_W ** -0.5),
        "a_conv_b": nrm((n_a, LRU_WIDTH), 0.01),
        "a_w_r": nrm((n_a, LRU_BLOCKS, LRU_BLOCK_W, LRU_BLOCK_W), LRU_BLOCK_W ** -0.5),
        "a_b_r": nrm((n_a, LRU_BLOCKS, LRU_BLOCK_W), 0.01),
        "a_w_i": nrm((n_a, LRU_BLOCKS, LRU_BLOCK_W, LRU_BLOCK_W), LRU_BLOCK_W ** -0.5),
        "a_b_i": nrm((n_a, LRU_BLOCKS, LRU_BLOCK_W), 0.01),
        "a_lam": jnp.log(a_dec) - jnp.log1p(-a_dec),
        "a_w_out": nrm((n_a, LRU_WIDTH, D_MODEL), LRU_WIDTH ** -0.5),
        "b_w_in": nrm((n_b, D_MODEL, DIL_IN_COLS), D_MODEL ** -0.5),
        "b_w_out": nrm((n_b, DIL_WIDTH, D_MODEL), DIL_WIDTH ** -0.5),
        "c_w_in": nrm((n_c, D_MODEL, NSA_IN_COLS), D_MODEL ** -0.5),
        "c_cmp_pos_k": nrm((n_c, CMP_BLOCK, NSA_HEAD_DIM), 0.1),
        "c_cmp_w1_k": nrm((n_c, CMP_BLOCK * NSA_HEAD_DIM, CMP_HIDDEN), (CMP_BLOCK * NSA_HEAD_DIM) ** -0.5),
        "c_cmp_w2_k": nrm((n_c, CMP_HIDDEN, NSA_HEAD_DIM), CMP_HIDDEN ** -0.5),
        "c_cmp_pos_v": nrm((n_c, CMP_BLOCK, NSA_HEAD_DIM), 0.1),
        "c_cmp_w1_v": nrm((n_c, CMP_BLOCK * NSA_HEAD_DIM, CMP_HIDDEN), (CMP_BLOCK * NSA_HEAD_DIM) ** -0.5),
        "c_cmp_w2_v": nrm((n_c, CMP_HIDDEN, NSA_HEAD_DIM), CMP_HIDDEN ** -0.5),
        "c_w_out": nrm((n_c, NSA_WIDTH, D_MODEL), NSA_WIDTH ** -0.5),
    }

def second_block(x, p, rel_bias, norm_pre, norm_post, ple_w_proj, ple_w_gate,
              a_w_in, a_conv_w, a_conv_b, a_w_r, a_b_r, a_w_i, a_b_i, a_lam, a_w_out,
              b_w_in, b_w_out,
              c_w_in, c_cmp_pos_k, c_cmp_w1_k, c_cmp_w2_k, c_cmp_pos_v, c_cmp_w1_v, c_cmp_w2_v, c_w_out):
    h = x
    for i in range(DEPTH_2):
        kind = i % N_MIXERS
        j = i // N_MIXERS
        u = _rmsnorm_2(h, norm_pre[i])
        if kind == 0:
            y = _rglru_mixer(u, a_w_in[j], a_conv_w[j], a_conv_b[j], a_w_r[j], a_b_r[j],
                             a_w_i[j], a_b_i[j], a_lam[j], a_w_out[j])
        elif kind == 1:
            y = _dilated_mixer(u, b_w_in[j], b_w_out[j], rel_bias)
        else:
            y = _nsa_mixer(u, c_w_in[j], c_cmp_pos_k[j], c_cmp_w1_k[j], c_cmp_w2_k[j],
                           c_cmp_pos_v[j], c_cmp_w1_v[j], c_cmp_w2_v[j], c_w_out[j], rel_bias)
        h = h + _rmsnorm_2(y, norm_post[i])
        h = h + jax.nn.sigmoid(h @ ple_w_gate[i]) * (p[i] @ ple_w_proj[i])
    return h


def setup_inputs(seed=0):
    out = dict(first_inputs(seed))
    for name, value in second_inputs(seed + 1).items():
        if name != "x":
            out[name + "_2"] = value
    return out


def reference(
    x, p, norm_g, w_in, conv_w, conv_b, cln_g, cln_b, sink, rel_bias, w_out, w_pe, pe_g, w_pg,
    final_g, p_2, rel_bias_2, norm_pre_2, norm_post_2, ple_w_proj_2, ple_w_gate_2, a_w_in_2,
    a_conv_w_2, a_conv_b_2, a_w_r_2, a_b_r_2, a_w_i_2, a_b_i_2, a_lam_2, a_w_out_2, b_w_in_2,
    b_w_out_2, c_w_in_2, c_cmp_pos_k_2, c_cmp_w1_k_2, c_cmp_w2_k_2, c_cmp_pos_v_2, c_cmp_w1_v_2,
    c_cmp_w2_v_2, c_w_out_2,
):
    x = first_block(
        x, p, norm_g, w_in, conv_w, conv_b, cln_g, cln_b, sink, rel_bias, w_out, w_pe, pe_g,
        w_pg, final_g,
    )
    return second_block(
        x, p_2, rel_bias_2, norm_pre_2, norm_post_2, ple_w_proj_2, ple_w_gate_2, a_w_in_2,
        a_conv_w_2, a_conv_b_2, a_w_r_2, a_b_r_2, a_w_i_2, a_b_i_2, a_lam_2, a_w_out_2,
        b_w_in_2, b_w_out_2, c_w_in_2, c_cmp_pos_k_2, c_cmp_w1_k_2, c_cmp_w2_k_2, c_cmp_pos_v_2,
        c_cmp_w1_v_2, c_cmp_w2_v_2, c_w_out_2,
    )


_drawn_inputs = setup_inputs


def setup_inputs(seed=0):
    import zlib

    import numpy as np

    out = dict(_drawn_inputs(seed))
    spreads = {}
    factors = {'norm_g': 5.199,
     'conv_b': 3.633,
     'cln_g': 6.242,
     'cln_b': 6.936,
     'sink': 8.0,
     'pe_g': 15.867,
     'a_b_r_2': 40.429,
     'a_b_i_2': 8.0,
     'a_conv_b_2': 2.743}
    for name, (base, spread) in spreads.items():
        noise = np.random.default_rng([zlib.crc32(name.encode()), seed]).standard_normal(out[name].shape)
        drawn = base * np.exp(spread * noise) if base else spread * noise
        out[name] = jnp.asarray(drawn.astype(out[name].dtype))
    for name, factor in factors.items():
        out[name] = (out[name] * factor).astype(out[name].dtype)
    return out
```

```python
import concourse.bass as bass
from concourse import mybir
from contextlib import ExitStack, contextmanager

D = 2048
S = 512
P = 128
NT = D // P
DEPTH = 2
WC = D // 2
CT = WC // P
DH = 64
HQ, HKV, GQ = 16, 4, 4
TAPS = 31
MID = TAPS // 2
BLK = 128
NB = S // BLK
PK = 2
TAPS2 = 4
EPS = 1e-6
NEG = -1e30
LRU_C = 8.0

UT = 8
UW = UT * P
RING = 4

A_U, KV_U, Z_U, OUT_U, PE_U, PG_U = 48, 8, 32, 32, 4, 32
A0 = 0
KV0 = A0 + A_U
Z0 = KV0 + KV_U
OUT0 = Z0 + Z_U
PE0 = OUT0 + OUT_U
PG0 = PE0 + PE_U
LAYER_U = PG0 + PG_U
B0 = DEPTH * LAYER_U
XB0 = B0
GT0 = XB0 + 32
RI0 = GT0 + 32
WO0 = RI0 + 8
WG0 = WO0 + 32
WP0 = WG0 + 32
UNITS = WP0 + 4

N_KV, N_Z, N_OUT, N_PG, LAYER_N = 24, 28, 44, 60, 76
NB0 = DEPTH * LAYER_N
PAIRS = HQ // 2 * NB

V_NORM, V_PEG, V_CB, V_LG, V_LB, V_SINK, V_CW = 0, 16, 32, 40, 48, 56, 72
LV_W = V_CW + CT * TAPS
W_FG, W_PRE, W_POST, W_CB, W_BR, W_BI, W_LAM, W_CW = (16 * i for i in range(8))
V2_W = W_CW + NT * TAPS2

A_STEPS = TAPS + 3
LAYER_STEPS = CT * A_STEPS + 200


class Steps:

    def __init__(self, eng, sem):
        self.eng, self.sem, self.base, self.n = eng, sem, 0, 0

    def did(self, ins):
        ins.then_inc(self.sem, 1)
        self.n += 1

    def settle(self, back=0):
        self.eng.wait_ge(self.sem, self.base + (self.n - back))

    @contextmanager
    def loop(self, lo, hi, per):
        base, n = self.base, self.n
        with self.eng.Fori(lo, hi) as i:
            self.base, self.n = base + (i * per + (n - lo * per) if per else n), 0
            yield i
            assert self.n == per, (self.n, per)
        self.base, self.n = base, n + per * (hi - lo)


def pair_of(n):
    kv, b, pr = n // 8, n % 8 // 2, n % 2
    lo, hi = max(0, b - 1), min(NB, b + 2)
    return kv, b, pr, kv % 2 * DH, kv // 2, lo, hi - lo


def build(nc, x, pin, lvec, vec2, relb, onehot, band, ident_in, w, out):
    F, R32 = mybir.dt.float32, mybir.dt.float32r
    ACT, ALU = mybir.ActivationFunctionType, mybir.AluOpType

    ctx = ExitStack()
    with ctx:
        def sb(name, cols, dt=F):
            return ctx.enter_context(nc.sbuf_tensor(name, [P, cols], dt))

        def sem(name):
            return ctx.enter_context(nc.semaphore(name))

        def tl(buf, t):
            return buf[:, bass.ds(t * S, S)]

        H = sb("H", NT * S)
        AR = 0
        PT = 2
        VT, KT, QT = 4, 6, 8
        XH = sb("XH", NT * S, R32)
        XL = sb("XL", NT * S, R32)
        raw = sb("raw", RING * UW)
        WH = sb("WH", RING * UW, R32)
        WL = sb("WL", RING * UW, R32)
        Y = sb("Y", NT * S)
        A2_COLS = 6 * S
        a2 = sb("a2", A2_COLS)
        T = sb("T", 6 * S)
        acc = sb("acc", S)
        rs = sb("rs", S)
        ident = sb("ident", P)
        ones = sb("ones", P)
        lv = sb("lv", LV_W)
        v2 = sb("v2", V2_W)
        der = sb("der", 3 * NT)
        sm = sb("sm", 3 * 12)
        eps = sb("eps", 1)

        praw = a2[:, 0:PK * S]
        PH, PL = (nc.alloc_sbuf_tensor_at(n, [P, PK * S], R32, offset=nc.lookup_mloc(a2).addr + (1 + i) * PK * S * 4)
                  for i, n in enumerate(("PH", "PL")))

        banks = [ctx.enter_context(nc.psum_tensor(n, [P, S], F))
                 for n in ("acc0", "acc1", "att", "stat", "sc0", "sc1", "tr0", "tr1")]
        G, VB, N, SC, TR = banks[0:2], banks[2], banks[3], banks[4:6], banks[6:8]
        SETS = [banks[0:4], banks[4:8]]

        h_spill = nc.dram_tensor("h_spill", [P, NT * S], F).ap()
        line_dram = nc.dram_tensor("bias_line", [HQ, S], F)
        bias_dram = nc.dram_tensor("bias_band", [HQ, P, 3 * BLK], F).ap()

        raw_in = [sem(f"raw_in{s}") for s in range(RING)]
        wh_ready = sem("wh_ready")
        wl_ready = sem("wl_ready")
        w_used = sem("w_used")
        h_in = [sem(f"h_in{c}") for c in range(4)]
        h_out = [sem(f"h_out{c}") for c in range(4)]
        const_in = sem("const_in")
        relb_in = sem("relb_in")
        lv_in = sem("lv_in")
        line_out = sem("line_out")
        bias_in = sem("bias_in")
        p_in = sem("p_in")
        out_sent = sem("out_sent")
        tile_out = sem("tile_out")
        h_ready = sem("h_ready")
        hsq_ready = sem("hsq_ready")
        hsum_ready = sem("hsum_ready")
        y_ready = sem("y_ready")
        xh_ready = sem("xh_ready")
        xl_ready = sem("xl_ready")
        stat_done = sem("stat_done")
        root_ready = sem("root_ready")
        init_done = sem("init_done")
        line_mm = sem("line_mm")
        line_ready = sem("line_ready")
        lam_exp = sem("lam_exp")
        lam_ready = sem("lam_ready")
        glu_th = sem("glu_th")
        ysum_ready = sem("ysum_ready")
        yc_ready = sem("yc_ready")
        ysq_ready = sem("ysq_ready")
        vsum_ready = sem("vsum_ready")
        ln_ready = sem("ln_ready")
        ln_th = sem("ln_th")
        vtr_done = sem("vtr_done")
        v_ready = sem("v_ready")
        z_th = sem("z_th")
        scores_done = sem("scores_done")
        scores_taken = sem("scores_taken")
        shift_ready = sem("shift_ready")
        exp_done = sem("exp_done")
        probs_ready = sem("probs_ready")
        tr_done = sem("tr_done")
        pt_ready = sem("pt_ready")
        pv_done = sem("pv_done")
        att_ready = sem("att_ready")
        ph_ready = sem("ph_ready")
        pl_ready = sem("pl_ready")
        e_out = sem("e_out")
        esq_ready = sem("esq_ready")
        esum_ready = sem("esum_ready")
        g_th = sem("g_th")
        x2_ready = sem("x2_ready")
        xsq_ready = sem("xsq_ready")
        xsum_ready = sem("xsum_ready")
        xc_ready = sem("xc_ready")
        gt_th = sem("gt_th")
        sg_ready = sem("sg_ready")
        ri_taken = sem("ri_taken")
        la_ready = sem("la_ready")
        lru_exp = sem("lru_exp")
        var_ready = sem("var_ready")
        lru_root = sem("lru_root")
        y2_ready = sem("y2_ready")
        osq_ready = sem("osq_ready")
        osum_ready = sem("osum_ready")
        h2_ready = sem("h2_ready")
        wg_th = sem("wg_th")
        proj_taken = sem("proj_taken")
        o_ready = sem("o_ready")
        dve_chain = sem("dve_chain")
        act_chain = sem("act_chain")

        CONSTS = 4
        block = ctx.enter_context(nc.Block())

        @block.sync
        def _(sp):
            def load(v, s):
                sp.dma_start(raw[:, s * UW:(s + 1) * UW],
                             w[bass.ds(v, 1)].rearrange("a p n -> (a p) n")).then_inc(raw_in[s], 16)

            def units(first, lo, hi):
                with sp.Fori(0, (hi - lo) // RING) as i:
                    for s in range(RING):
                        v = first + (i * RING + (lo + s))
                        sp.wait_ge(wl_ready, v + 1)
                        load(v + RING, s)

            def h_dma(c, store):
                part = slice(c * 4 * S, (c + 1) * 4 * S)
                if store:
                    sp.dma_start(h_spill[:, part], H[:, part]).then_inc(h_out[c], 16)
                else:
                    sp.dma_start(H[:, part], h_spill[:, part]).then_inc(h_in[c], 16)

            def load_bias(kv):
                sp.dma_start(a2[:, 3 * S:6 * S].rearrange("p (g k) -> p g k", g=GQ),
                             bias_dram[kv * GQ:(kv + 1) * GQ].rearrange("g q k -> q g k")).then_inc(bias_in, 16)

            sp.dma_start(ones[0:32, 0:HQ], relb).then_inc(relb_in, 16)
            sp.dma_start(T[0:32, 0:S], onehot).then_inc(relb_in, 16)
            sp.dma_start(T[0:HQ, S:2 * S], band).then_inc(relb_in, 16)
            sp.dma_start(ident[:, :], ident_in).then_inc(const_in, 16)
            sp.dma_start(v2[:, :], vec2).then_inc(const_in, 16)
            for c in range(4):
                sp.dma_start(H[:, c * 4 * S:(c + 1) * 4 * S], x[:, c * 4 * S:(c + 1) * 4 * S]).then_inc(h_in[c], 16)
            for s in range(RING):
                load(s, s)
            sp.wait_ge(line_ready, 1)
            sp.dma_start(line_dram.ap(), T[0:HQ, 2 * S:3 * S]).then_inc(line_out, 16)
            sp.wait_ge(line_out, 16)
            sp.dma_start(bias_dram, bass.AP(line_dram, P - 1, [[S, HQ], [-1, P], [1, 3 * BLK]])).then_inc(line_out, 16)
            sp.wait_ge(line_out, 32)

            with sp.Fori(0, DEPTH) as ly:
                u0 = ly * LAYER_U
                units(u0, 0, 4)
                sp.wait_ge(hsum_ready, ly * NT + NT)
                sp.dma_start(lv[:, :], lvec[bass.ds(ly, 1)].rearrange("a p n -> (a p) n")).then_inc(lv_in, 16)
                for c in range(4):
                    h_dma(c, True)
                load_bias(0)
                units(u0, 4, Z0 + 8)
                for kv in range(1, HKV):
                    sp.wait_ge(scores_taken, ly * (2 * PAIRS) + 16 * kv)
                    load_bias(kv)
                    units(u0, Z0 + 8 * kv, Z0 + 8 * kv + 8)
                sp.wait_ge(y_ready, ly * NT + NT)
                for c in range(4):
                    sp.wait_ge(h_out[c], ly * 16 + 16)
                    h_dma(c, False)
                units(u0, OUT0, OUT0 + 8)
                sp.wait_ge(tr_done, ly * (2 * PAIRS) + 2 * PAIRS)
                sp.dma_start(praw, pin[bass.ds(ly, 1)].rearrange("a p n -> (a p) n")).then_inc(p_in, 16)
                units(u0, OUT0 + 8, LAYER_U)

            units(B0, 0, 16)
            sp.wait_ge(x2_ready, NT)
            for c in range(4):
                h_dma(c, True)
            units(B0, 16, 84)
            sp.wait_ge(y2_ready, NT)
            for c in range(4):
                sp.wait_ge(h_out[c], DEPTH * 16 + 16)
                h_dma(c, False)
            sp.dma_start(praw, pin[DEPTH]).then_inc(p_in, 16)
            units(B0, 84, UNITS - B0 - RING)
            for c in range(4):
                sp.wait_ge(o_ready, 4 * c + 4)
                sp.dma_start(out[:, c * 4 * S:(c + 1) * 4 * S], H[:, c * 4 * S:(c + 1) * 4 * S]).then_inc(out_sent, 16)
            sp.wait_ge(out_sent, 4 * 16)

        @block.gpsimd
        def _(pool):
            with pool.Fori(0, UNITS // RING) as i:
                for s in range(RING):
                    pool.wait_ge(wh_ready, i * RING + (s + 1))
                    c = slice(s * UW, (s + 1) * UW)
                    pool.tensor_tensor(WL[:, c], raw[:, c], WH[:, c].bitcast(F),
                                       ALU.subtract).then_inc(wl_ready, 1)

        @block.scalar
        def _(act):
            chain = Steps(act, act_chain)

            def high(s):
                c = slice(s * UW, (s + 1) * UW)
                act.activation(WH[:, c], raw[:, c], ACT.Copy).then_inc(wh_ready, 1)

            def prep(first, v):
                act.wait_ge(raw_in[v % RING], first * (16 // RING) + 16 * (v // RING + 2))
                act.wait_ge(w_used, first + (v + 1))
                high(v % RING)

            def prep_loop(first, lo, n, i, per):
                act.wait_ge(raw_in[n % RING], first * (16 // RING) + (i * (16 * per // RING) + 16 * ((lo + n) // RING + 2)))
                act.wait_ge(w_used, first + (i * per + (lo + n + 1)))
                high(n % RING)

            def preps(first, lo, hi):
                with act.Fori(0, (hi - lo) // RING) as i:
                    for s in range(RING):
                        prep_loop(first, lo, s, i, RING)

            def xhigh(t, src, scale=1.0):
                act.activation(tl(XH, t), src, ACT.Copy, scale=scale).then_inc(xh_ready, 1)

            def root(dst, count, mean):
                act.wait_ge(stat_done, count)
                act.activation(dst, N[:, :], ACT.Sqrt, bias=eps[:, 0:1], scale=mean).then_inc(root_ready, 1)

            for s in range(RING):
                act.wait_ge(raw_in[s], 16)
                high(s)
            act.wait_ge(lam_ready, 1)
            act.activation(T[:, 3 * S:3 * S + NT], T[:, 3 * S:3 * S + NT], ACT.Exp, scale=-1.0).then_inc(lam_exp, 1)

            with act.Fori(0, DEPTH) as ly:
                u0 = ly * LAYER_U
                n0 = ly * LAYER_N

                act.wait_ge(lv_in, ly * 16 + 16)
                act.wait_ge(hsum_ready, ly * NT + NT)
                for t in range(NT):
                    xhigh(t, tl(H, t), lv[:, V_NORM + t:V_NORM + t + 1])
                root(rs[:, :], ly * 4 + 1, 1.0 / D)

                with act.Fori(0, CT // 2) as i:
                    for h in range(2):
                        for k in range(6):
                            prep_loop(u0, A0, 6 * h + k, i, 12)
                            if k == 2:
                                act.wait_ge(tile_out, n0 + (i * 6 + (3 * h + 1 + 2)))
                                act.activation(tl(T, h), tl(T, h), ACT.Tanh).then_inc(glu_th, 1)

                prep(u0, KV0)
                prep(u0, KV0 + 1)
                prep(u0, KV0 + 2)
                prep(u0, KV0 + 3)
                for t in range(CT):
                    act.wait_ge(yc_ready, ly * CT + (t + 1))
                    if t >= 2:
                        act.wait_ge(vsum_ready, ly * CT + (t - 1))
                    act.activation(tl(T, t % 2), tl(Y, t), ACT.Square).then_inc(ysq_ready, 1)
                    if t in (3, 7):
                        prep(u0, KV0 + 4 + t // 4)
                prep(u0, KV0 + 6)
                prep(u0, KV0 + 7)
                root(tl(T, 4), ly * 4 + 3, 1.0 / WC)
                for j in range(2):
                    act.wait_ge(vtr_done, ly * 2 + (j + 1))
                    act.activation(H[:, VT * S:(VT + 2) * S].rearrange("p (t c) -> p t c", t=NB)[:, :, j * P:(j + 1) * P],
                                   TR[j][:, :].rearrange("p (t c) -> p t c", t=NB), ACT.Copy).then_inc(v_ready, 1)
                for t in range(CT):
                    act.wait_ge(ln_ready, ly * CT + (t + 1))
                    act.activation(tl(T, t % 2), tl(Y, t), ACT.Tanh).then_inc(ln_th, 1)

                def exps(n):
                    st = sm[:, 12 * (n % 3):12 * (n % 3) + 12]
                    keys = pair_of(n)[6] * BLK
                    act.wait_ge(shift_ready, ly * PAIRS + (n + 1))
                    for hh in range(2):
                        pb = pbuf(n)[:, hh * 3 * BLK:hh * 3 * BLK + keys]
                        act.activation(pb, pb, ACT.Exp, bias=st[:, 2 + hh:3 + hh], accum_out=st[:, 6 + hh:7 + hh])
                    act.activation(st[:, 8:10], st[:, 4:6], ACT.Exp).then_inc(exp_done, 1)

                def pbuf(n):
                    return H[:, AR * S:AR * S + 6 * BLK] if n % 3 == 2 else a2[:, n % 3 * 6 * BLK:(n % 3 + 1) * 6 * BLK]

                def probs_out(n):
                    nk = pair_of(n)[6]
                    if n:
                        act.wait_ge(pv_done, ly * PAIRS + n)
                    pt = H[:, PT * S:PT * S + 6 * BLK].rearrange("p (k h q) -> p k h q", k=3, h=2)
                    for hh in range(2):
                        act.wait_ge(tr_done, ly * (2 * PAIRS) + (2 * n + hh + 1))
                        act.activation(pt[:, 0:nk, hh, :], TR[hh][:, 0:nk * BLK].rearrange("p (k q) -> p k q", k=nk),
                                       ACT.Copy).then_inc(pt_ready, 1)

                for n in range(PAIRS + 2):
                    if n < PAIRS:
                        prep(u0, Z0 + n)
                        if n % 2 == 1:
                            j = n // 2
                            act.wait_ge(tile_out, n0 + (N_Z + j + 1 + 2))
                            act.activation(tl(T, 2 + j % 2), tl(T, j % 2), ACT.Tanh).then_inc(z_th, 1)
                        exps(n)
                    if n >= 2:
                        probs_out(n - 2)

                act.wait_ge(w_used, u0 + OUT0)
                for t in range(NT):
                    act.wait_ge(y_ready, ly * NT + (t + 1))
                    xhigh(t, tl(Y, t))
                preps(u0, OUT0, OUT0 + 16)
                act.wait_ge(p_in, ly * 16 + 16)
                act.activation(PH[:, :], praw, ACT.Copy).then_inc(ph_ready, 1)
                preps(u0, OUT0 + 16, PE0)

                for t in range(NT):
                    if t % 4 == 0:
                        prep(u0, PE0 + t // 4)
                    act.activation(tl(Y, t), SETS[t // 4 % 2][t % 4][:, :], ACT.Copy, scale=0.5).then_inc(e_out, 1)
                    if t == 0:
                        act.wait_ge(tile_out, n0 + (N_PG + 2))
                    xhigh(t, tl(H, t))
                for t in range(NT):
                    if t % 8 == 0:
                        prep(u0, PG0 + t // 8)
                    if t == 0:
                        act.wait_ge(e_out, ly * NT + NT)
                    if t >= 2:
                        act.wait_ge(esum_ready, ly * NT + (t - 1))
                    act.activation(tl(T, 2 + t % 2), tl(Y, t), ACT.Square).then_inc(esq_ready, 1)
                prep(u0, PG0 + 2)
                prep(u0, PG0 + 3)
                root(rs[:, :], ly * 4 + 4, 4.0 / D)

                def gate(first, j, slot, i=0):
                    act.wait_ge(tile_out, n0 + (i * 2 + (N_PG + first + j + 1 + 2)))
                    act.activation(tl(T, slot), tl(T, slot), ACT.Tanh).then_inc(g_th, 1)

                def square(first, j, slot, i=0):
                    act.wait_ge(h_ready, ly * NT + (i * 2 + (first + j + 1)))
                    act.activation(tl(T, 2 + slot), tl(H, i * 2 + (first + j)), ACT.Square).then_inc(hsq_ready, 1)

                gate(0, 0, 0)
                gate(0, 1, 1)
                square(0, 0, 0)
                square(0, 1, 1)
                with act.Fori(0, NT // 2 - 1) as i:
                    for j in range(2):
                        prep_loop(u0, PG0 + 4, 2 * j, i, 4)
                        prep_loop(u0, PG0 + 4, 2 * j + 1, i, 4)
                        gate(2, j, j, i)
                        act.wait_ge(hsum_ready, ly * NT + (i * 2 + (NT + 2 + j - 1)))
                        square(2, j, j, i)

            root(rs[:, :], DEPTH * 4 + 1, 1.0 / D)
            for t in range(NT):
                act.wait_ge(x2_ready, t + 1)
                xhigh(t, tl(H, t), v2[:, W_PRE + t:W_PRE + t + 1])
            for t in range(NT):
                if t >= 2:
                    act.wait_ge(xsum_ready, t - 1)
                act.activation(tl(T, t % 2), tl(H, t), ACT.Square).then_inc(xsq_ready, 1)
                if t % 4 == 3:
                    prep(B0, t // 4)
            root(rs[:, :], DEPTH * 4 + 2, 1.0 / D)
            preps(B0, 4, GT0 - B0)
            with act.Fori(0, NT // 2) as i:
                for j in range(2):
                    prep_loop(B0, GT0 - B0, 2 * j, i, 4)
                    prep_loop(B0, GT0 - B0, 2 * j + 1, i, 4)
                    act.wait_ge(tile_out, i * 2 + (NB0 + 16 + j + 1 + 2))
                    act.activation(tl(T, 2 + j), tl(T, j), ACT.Tanh).then_inc(gt_th, 1)

            for t in range(NT):
                act.wait_ge(xc_ready, t + 1)
                if t == 0:
                    act.wait_ge(w_used, RI0)
                xhigh(t, tl(Y, t))

            def slots(n):
                b = a2 if n % 2 == 0 else T
                return [[tl(b, 2 * q + m) for m in range(2)] for q in range(3)]

            def tanhs(n):
                la, ti, _ = slots(n)
                prep(B0, RI0 - B0 + n)
                for q, dst in ((0, la), (1, ti)):
                    for m in range(2):
                        if n >= 2:
                            act.wait_ge(y2_ready, 2 * n - 2)
                        act.activation(dst[m], SETS[n % 2][2 * q + m][:, :], ACT.Tanh, scale=0.5,
                                       bias=der[:, (1 + q) * NT + 2 * n + m:(1 + q) * NT + 2 * n + m + 1]).then_inc(ri_taken, 1)

            def decays(n):
                la, ti, a = slots(n)
                act.wait_ge(la_ready, 4 * n + 4)
                for m in range(2):
                    act.activation(a[m], la[m], ACT.Exp).then_inc(lru_exp, 1)
                for m in range(2):
                    act.activation(la[m], la[m], ACT.Tanh, scale=-1.0).then_inc(lru_exp, 1)
                act.wait_ge(lru_exp, 6 * n + 2)
                for m in range(2):
                    act.activation(ti[m], a[m], ACT.Square).then_inc(lru_exp, 1)

            def roots(n):
                la, _, _ = slots(n)
                act.wait_ge(var_ready, 2 * n + 2)
                for m in range(2):
                    act.activation(la[m], la[m], ACT.Sqrt).then_inc(lru_root, 1)

            def yhigh(n):
                for m in range(2):
                    act.wait_ge(y2_ready, 2 * n + m + 1)
                    xhigh(2 * n + m, tl(Y, 2 * n + m))

            tanhs(0)
            for n in range(8):
                decays(n)
                if n < 7:
                    tanhs(n + 1)
                if n:
                    yhigh(n - 1)
                roots(n)
            yhigh(7)

            with act.Fori(0, NT // 2) as i:
                for j in range(2):
                    prep_loop(B0, WO0 - B0, 2 * j, i, 4)
                    prep_loop(B0, WO0 - B0, 2 * j + 1, i, 4)
                    act.wait_ge(tile_out, i * 2 + (NB0 + 32 + j + 1 + 2))
                    act.activation(tl(T, j), tl(Y, i * 2 + j), ACT.Square).then_inc(osq_ready, 1)
            root(rs[:, :], DEPTH * 4 + 3, 1.0 / D)
            act.wait_ge(p_in, DEPTH * 16 + 16)
            act.activation(PH[:, :], praw, ACT.Copy).then_inc(ph_ready, 1)
            for t in range(NT):
                act.wait_ge(h2_ready, t + 1)
                xhigh(t, tl(H, t))
            with act.Fori(0, NT // 2) as i:
                for j in range(2):
                    prep_loop(B0, WG0 - B0, 2 * j, i, 4)
                    prep_loop(B0, WG0 - B0, 2 * j + 1, i, 4)
                    act.wait_ge(tile_out, i * 2 + (NB0 + 48 + j + 1 + 2))
                    act.activation(tl(Y, i * 2 + j), tl(T, j), ACT.Tanh).then_inc(wg_th, 1)

        @block.vector
        def _(dve):
            chain = Steps(dve, dve_chain)
            did, settle = chain.did, chain.settle

            def col(v, c):
                return v[:, bass.ds(c, 1)]

            def stt(out_, in0, scalar, in1, op0, op1):
                return dve.scalar_tensor_tensor(out_, in0, scalar, in1, op0, op1)

            def xlow(t, src, count, scale=1.0):
                dve.wait_ge(xh_ready, count)
                stt(tl(XL, t), src, scale, tl(XH, t).bitcast(F), ALU.mult, ALU.subtract).then_inc(xl_ready, 1)

            def inv_rms(dst, count):
                dve.wait_ge(root_ready, count)
                did(dve.reciprocal(dst, dst))

            dve.memset(eps[:, :], EPS).then_inc(tile_out, 1)
            dve.memset(acc[:, :], 0.0).then_inc(tile_out, 1)
            dve.wait_ge(line_mm, 1)
            dve.tensor_tensor(T[0:HQ, 2 * S:3 * S], SC[0][0:HQ, :], T[0:HQ, S:2 * S], ALU.add).then_inc(line_ready, 1)
            dve.memset(ones[:, :], 1.0).then_inc(init_done, 1)
            dve.wait_ge(const_in, 32)
            lam = v2[:, W_LAM:W_LAM + NT]
            e_, s_, q_, p_ = (T[:, 3 * S + NT * i:3 * S + NT * (i + 1)] for i in range(4))
            did(dve.tensor_scalar(q_, lam, -1.0, None, ALU.mult))
            settle()
            dve.tensor_tensor(e_, lam, q_, ALU.max).then_inc(lam_ready, 1)
            did(dve.tensor_scalar(der[:, NT:2 * NT], v2[:, W_BR:W_BR + NT], 0.5, None, ALU.mult))
            did(dve.tensor_scalar(der[:, 2 * NT:3 * NT], v2[:, W_BI:W_BI + NT], 0.5, None, ALU.mult))
            dve.wait_ge(lam_exp, 1)
            did(dve.tensor_scalar(s_, e_, 2.0, None, ALU.add))
            settle()
            did(dve.reciprocal(s_, s_))
            settle()
            did(dve.tensor_tensor(s_, s_, e_, ALU.mult))
            settle()
            did(dve.tensor_tensor(q_, s_, s_, ALU.mult))
            settle()
            TERMS = 9
            did(dve.tensor_scalar(p_, q_, 1.0 / (2 * TERMS + 1), 1.0 / (2 * TERMS - 1), ALU.mult, ALU.add))
            settle()
            for k in range(TERMS - 2, -1, -1):
                did(dve.tensor_tensor(p_, p_, q_, ALU.mult))
                settle()
                did(dve.tensor_scalar(p_, p_, 1.0 / (2 * k + 1), None, ALU.add))
                settle()
            did(stt(p_, p_, 2.0, s_, ALU.mult, ALU.mult))
            did(dve.tensor_scalar(q_, lam, -1.0, 0.0, ALU.mult, ALU.max))
            settle()
            did(dve.tensor_tensor(p_, p_, q_, ALU.add))
            settle()
            did(dve.tensor_scalar(der[:, 0:NT], p_, -LRU_C / 2, None, ALU.mult))
            dve.wait_ge(tile_out, 2)
            for t in range(NT):
                if t % 4 == 0:
                    dve.wait_ge(h_in[t // 4], 16)
                did(dve.tensor_tensor(tl(T, 4 + t % 2), tl(H, t), tl(H, t), ALU.mult))
                settle()
                if t:
                    dve.wait_ge(hsum_ready, t)
                dve.tensor_tensor(acc[:, :], acc[:, :], tl(T, 4 + t % 2), ALU.add).then_inc(hsum_ready, 1)

            with chain.loop(0, DEPTH, LAYER_STEPS) as ly:
                u0 = ly * LAYER_U
                n0 = ly * LAYER_N
                x0 = ly * (3 * NT)

                def taken(n):
                    dve.wait_ge(w_used, u0 + n)

                for t in range(NT):
                    xlow(t, tl(H, t), x0 + (t + 1), lv[:, V_NORM + t:V_NORM + t + 1])
                inv_rms(rs[:, :], ly * 3 + 1)
                settle()
                for c in range(4):
                    dve.wait_ge(h_out[c], ly * 16 + 16)
                did(dve.memset(acc[:, :], 0.0))

                with chain.loop(0, CT // 2, 2 * A_STEPS) as i:
                    for h in range(2):
                        t = i * 2 + h
                        u = i * 12 + 6 * h
                        n = i * 6 + 3 * h
                        a = tl(H, AR + h)
                        y = tl(Y, t)
                        taken(u + 2)
                        stt(tl(T, h), G[h % 2][:, :], 0.5, rs[:, :], ALU.mult, ALU.mult).then_inc(tile_out, 1)
                        taken(u + 4)
                        stt(tl(T, 2), G[(h + 1) % 2][:, :], 0.5, rs[:, :], ALU.mult, ALU.mult).then_inc(tile_out, 1)
                        dve.wait_ge(glu_th, ly * CT + (t + 1))
                        dve.wait_ge(tile_out, n0 + (n + 2 + 2))
                        did(stt(a, tl(T, h), 1.0, tl(T, 2), ALU.add, ALU.mult))
                        settle()
                        wcol = lambda j: col(lv, t * TAPS + (V_CW + j))
                        did(dve.tensor_scalar(y, a, wcol(MID), col(lv, t + V_CB), ALU.mult, ALU.add))
                        c2 = tl(T, 3)
                        did(dve.memset(c2, 0.0))
                        side = [j for j in range(TAPS) if j != MID]
                        for k, j in enumerate(side):
                            lo, hi = max(0, MID - j), min(S, S + MID - j)
                            dst = y if k % 2 == 0 else c2
                            settle(1)
                            did(stt(dst[:, lo:hi], a[:, lo + j - MID:hi + j - MID], wcol(j), dst[:, lo:hi],
                                    ALU.mult, ALU.add))
                            if k == 18:
                                taken(u + 6)
                                stt(tl(H, t + QT), G[h % 2][:, :], DH ** -0.5, rs[:, :],
                                    ALU.mult, ALU.mult).then_inc(tile_out, 1)
                        settle()
                        did(dve.tensor_tensor(y, y, c2, ALU.add))
                        settle()
                        dve.tensor_tensor(acc[:, :], acc[:, :], y, ALU.add).then_inc(ysum_ready, 1)
                        dve.wait_ge(ysum_ready, ly * CT + (t + 1))

                for j in range(2):
                    taken(KV0 + 2 * j + 2)
                    dve.tensor_tensor(tl(H, KT + j), G[j][:, :], rs[:, :], ALU.mult).then_inc(tile_out, 1)
                dve.wait_ge(stat_done, ly * 4 + 2)
                did(dve.tensor_scalar(tl(T, 4), N[:, :], 1.0 / WC, None, ALU.mult))
                did(dve.memset(acc[:, :], 0.0))
                settle()
                for t in range(CT):
                    dve.tensor_tensor(tl(Y, t), tl(Y, t), tl(T, 4), ALU.subtract).then_inc(yc_ready, 1)

                def vsum(t):
                    dve.wait_ge(ysq_ready, ly * CT + (t + 1))
                    if t:
                        dve.wait_ge(vsum_ready, ly * CT + t)
                    dve.tensor_tensor(acc[:, :], acc[:, :], tl(T, t % 2), ALU.add).then_inc(vsum_ready, 1)

                for t in range(CT):
                    vsum(t)
                for j in range(2):
                    taken(KV0 + 4 + 2 * j + 2)
                    dve.tensor_tensor(tl(H, PT + j), G[j][:, :], rs[:, :], ALU.mult).then_inc(tile_out, 1)
                inv_rms(tl(T, 4), ly * 3 + 2)
                settle()
                for t in range(CT):
                    did(stt(tl(Y, t), tl(Y, t), lv[:, V_LG + t:V_LG + t + 1], tl(T, 4), ALU.mult, ALU.mult))
                for t in range(CT):
                    if t == 0:
                        settle()
                    dve.tensor_scalar(tl(Y, t), tl(Y, t), lv[:, V_LB + t:V_LB + t + 1], 0.5, ALU.add,
                                      ALU.mult).then_inc(ln_ready, 1)
                    if t:
                        dve.wait_ge(ln_th, ly * CT + t)
                        did(stt(tl(Y, t - 1), tl(T, (t - 1) % 2), 1.0, tl(Y, t - 1), ALU.add, ALU.mult))
                dve.wait_ge(ln_th, ly * CT + CT)
                did(stt(tl(Y, CT - 1), tl(T, (CT - 1) % 2), 1.0, tl(Y, CT - 1), ALU.add, ALU.mult))

                def pbuf(n):
                    return H[:, AR * S:AR * S + 6 * BLK] if n % 3 == 2 else a2[:, n % 3 * 6 * BLK:(n % 3 + 1) * 6 * BLK]

                def stats(n):
                    return sm[:, 12 * (n % 3):12 * (n % 3) + 12]

                def scores(n):
                    kv, b, pr, _, _, lo, nk = pair_of(n)
                    st = stats(n)
                    if n % 8 == 0:
                        dve.wait_ge(bias_in, ly * (16 * HKV) + 16 * (kv + 1))
                    h0 = V_SINK + kv * GQ + 2 * pr
                    dve.wait_ge(scores_done, ly * (2 * PAIRS) + (2 * n + 2))
                    did(dve.tensor_copy(st[:, 4:6], lv[:, h0:h0 + 2]))
                    for hh in range(2):
                        g = 2 * pr + hh
                        off = 3 * S + g * 3 * BLK + (BLK if b == 0 else 0)
                        dve.tensor_tensor_reduce(pbuf(n)[:, hh * 3 * BLK:hh * 3 * BLK + nk * BLK],
                                                 SC[hh][:, 0:nk * BLK], a2[:, off:off + nk * BLK], 1.0,
                                                 lv[:, V_SINK + kv * GQ + g:V_SINK + kv * GQ + g + 1],
                                                 ALU.add, ALU.max, st[:, hh:hh + 1]).then_inc(scores_taken, 1)
                    dve.wait_ge(scores_taken, ly * (2 * PAIRS) + (2 * n + 2))
                    did(dve.tensor_scalar(st[:, 2:4], st[:, 0:2], -1.0, None, ALU.mult))
                    dve.tensor_tensor(st[:, 4:6], st[:, 4:6], st[:, 0:2], ALU.subtract).then_inc(shift_ready, 1)

                def finish(n):
                    st = stats(n)
                    keys = pair_of(n)[6] * BLK
                    dve.wait_ge(exp_done, ly * PAIRS + (n + 1))
                    did(dve.tensor_tensor(st[:, 10:12], st[:, 6:8], st[:, 8:10], ALU.add))
                    settle()
                    did(dve.reciprocal(st[:, 10:12], st[:, 10:12]))
                    settle()
                    for hh in range(2):
                        pb = pbuf(n)[:, hh * 3 * BLK:hh * 3 * BLK + keys]
                        ins = dve.tensor_scalar(pb, pb, st[:, 10 + hh:11 + hh], None, ALU.mult)
                        ins.then_inc(probs_ready, 1)

                def att_out(n):
                    kv, b, pr, r0, kvp, _, _ = pair_of(n)
                    dve.wait_ge(pv_done, ly * PAIRS + (n + 1))
                    q = H[r0:r0 + DH, (QT + 4 * kvp + 2 * pr) * S:(QT + 4 * kvp + 2 * pr + 2) * S]
                    dve.tensor_copy(q.rearrange("p (g s) -> p g s", g=2)[:, :, b * BLK:(b + 1) * BLK],
                                    VB[r0:r0 + DH, 0:2 * BLK].rearrange("p (g s) -> p g s", g=2)).then_inc(att_ready, 1)

                for n in range(PAIRS + 3):
                    if 1 <= n <= PAIRS:
                        finish(n - 1)
                    if n < PAIRS:
                        scores(n)
                    if n % 2 == 0 and 2 <= n <= PAIRS:
                        j = n // 2 - 1
                        dve.wait_ge(z_th, ly * NT + (j + 1))
                        zg = stt(tl(T, j % 2) if j < CT else tl(Y, j), tl(T, 2 + j % 2), 1.0, tl(T, j % 2),
                                 ALU.add, ALU.mult)
                        did(zg)
                        if j < CT:
                            settle()
                            dve.tensor_tensor(tl(Y, j), tl(Y, j), tl(T, j % 2), ALU.mult).then_inc(y_ready, 1)
                    if n < PAIRS and n % 2 == 1:
                        j = n // 2
                        taken(Z0 + 2 * j + 2)
                        stt(tl(T, j % 2), G[j % 2][:, :], 0.5, rs[:, :], ALU.mult, ALU.mult).then_inc(tile_out, 1)
                    if n >= 3:
                        att_out(n - 3)
                settle()
                dve.wait_ge(att_ready, ly * PAIRS + PAIRS)
                for t in range(CT):
                    dve.tensor_tensor(tl(Y, CT + t), tl(Y, CT + t), tl(H, QT + t), ALU.mult).then_inc(y_ready, 1)

                for t in range(NT):
                    xlow(t, tl(Y, t), x0 + (NT + t + 1))

                def add_out(i, j):
                    t = i * 2 + j
                    for c in range(4):
                        dve.wait_ge(h_in[c], ly * 16 + 32)
                    taken(i * 4 + (OUT0 + 2 * j + 2))
                    dve.tensor_tensor(tl(H, t), tl(H, t), G[j][:, :], ALU.add).then_inc(tile_out, 1)

                with chain.loop(0, 4, 0) as i:
                    for j in range(2):
                        add_out(i, j)
                dve.wait_ge(ph_ready, ly + 1)
                dve.tensor_tensor(PL[:, :], praw, PH[:, :].bitcast(F), ALU.subtract).then_inc(pl_ready, 1)
                with chain.loop(4, 8, 0) as i:
                    for j in range(2):
                        add_out(i, j)

                dve.wait_ge(tile_out, n0 + (N_PG + 2))
                for t in range(NT):
                    xlow(t, tl(H, t), x0 + (2 * NT + t + 1))
                did(dve.memset(acc[:, :], 0.0))
                settle()
                for t in range(NT):
                    dve.wait_ge(esq_ready, ly * NT + (t + 1))
                    if t:
                        dve.wait_ge(esum_ready, ly * NT + t)
                    dve.tensor_tensor(acc[:, :], acc[:, :], tl(T, 2 + t % 2), ALU.add).then_inc(esum_ready, 1)

                def halve(t0, j, i=0):
                    taken(i * 4 + (PG0 + 2 * (t0 + j) + 2))
                    dve.tensor_scalar(tl(T, j), G[j][:, :], 0.5, None, ALU.mult).then_inc(tile_out, 1)

                def gated(t0, j, i=0):
                    t = i * 2 + (t0 + j)
                    dve.wait_ge(g_th, ly * NT + (i * 2 + (t0 + j + 1)))
                    did(stt(tl(T, j), tl(T, j), 1.0, tl(Y, t), ALU.add, ALU.mult))
                    settle()
                    did(stt(tl(T, j), tl(T, j), col(lv, t + V_PEG), rs[:, :], ALU.mult, ALU.mult))
                    settle()
                    dve.tensor_tensor(tl(H, t), tl(H, t), tl(T, j), ALU.add).then_inc(h_ready, 1)

                def hsum(t0, j, i=0):
                    dve.wait_ge(hsq_ready, ly * NT + (i * 2 + (t0 + j + 1)))
                    dve.wait_ge(hsum_ready, ly * NT + (i * 2 + (NT + t0 + j)))
                    dve.tensor_tensor(acc[:, :], acc[:, :], tl(T, 2 + j), ALU.add).then_inc(hsum_ready, 1)

                halve(0, 0)
                halve(0, 1)
                inv_rms(rs[:, :], ly * 3 + 3)
                did(dve.memset(acc[:, :], 0.0))
                settle()
                gated(0, 0)
                gated(0, 1)
                with chain.loop(0, NT // 2 - 1, 4) as i:
                    for j in range(2):
                        halve(2, j, i)
                        hsum(0, j, i)
                        gated(2, j, i)
                hsum(NT - 2, 0)
                hsum(NT - 2, 1)

            xb = DEPTH * 3 * NT
            inv_rms(rs[:, :], DEPTH * 3 + 1)
            did(dve.memset(acc[:, :], 0.0))
            settle()
            for t in range(NT):
                stt(tl(H, t), tl(H, t), v2[:, W_FG + t:W_FG + t + 1], rs[:, :], ALU.mult, ALU.mult).then_inc(x2_ready, 1)
                if t:
                    xlow(t - 1, tl(H, t - 1), xb + t, v2[:, W_PRE + t - 1:W_PRE + t])
            xlow(NT - 1, tl(H, NT - 1), xb + NT, v2[:, W_PRE + NT - 1:W_PRE + NT])
            for t in range(NT):
                dve.wait_ge(xsq_ready, t + 1)
                if t:
                    dve.wait_ge(xsum_ready, t)
                dve.tensor_tensor(acc[:, :], acc[:, :], tl(T, t % 2), ALU.add).then_inc(xsum_ready, 1)
            inv_rms(rs[:, :], DEPTH * 3 + 2)
            settle()

            with chain.loop(0, NT // 2, 2 * (TAPS2 - 1)) as i:
                for j in range(2):
                    t = i * 2 + j
                    dve.wait_ge(w_used, i * 4 + (XB0 + 2 * j + 2))
                    dve.tensor_tensor(tl(T, j), G[j][:, :], rs[:, :], ALU.mult).then_inc(tile_out, 1)
                    dve.wait_ge(tile_out, i * 2 + (NB0 + j + 1 + 2))
                    y = tl(Y, t)
                    did(dve.tensor_scalar(y, tl(T, j), col(v2, t * TAPS2 + (W_CW + TAPS2 - 1)), col(v2, t + W_CB),
                                          ALU.mult, ALU.add))
                    for k in range(TAPS2 - 2, -1, -1):
                        back = TAPS2 - 1 - k
                        settle()
                        ins = stt(y[:, back:S], tl(T, j)[:, 0:S - back], col(v2, t * TAPS2 + (W_CW + k)), y[:, back:S],
                                  ALU.mult, ALU.add)
                        if k:
                            did(ins)
                        else:
                            ins.then_inc(xc_ready, 1)

            for c in range(4):
                dve.wait_ge(h_out[c], DEPTH * 16 + 16)
            with chain.loop(0, NT // 2, 0) as i:
                for j in range(2):
                    dve.wait_ge(w_used, i * 4 + (GT0 + 2 * j + 2))
                    stt(tl(T, j), G[j][:, :], 0.5, rs[:, :], ALU.mult, ALU.mult).then_inc(tile_out, 1)
                    dve.wait_ge(gt_th, i * 2 + (j + 1))
                    stt(tl(H, i * 2 + j), tl(T, 2 + j), 1.0, tl(T, j), ALU.add, ALU.mult).then_inc(sg_ready, 1)

            for t in range(NT):
                xlow(t, tl(Y, t), xb + NT + t + 1)

            def slots(n):
                b = a2 if n % 2 == 0 else T
                return [[tl(b, 2 * q + m) for m in range(2)] for q in range(3)]

            def inputs(n):
                la, ti, _ = slots(n)
                dve.wait_ge(ri_taken, 4 * n + 4)
                for m in range(2):
                    dve.tensor_scalar(la[m], la[m], 1.0, der[:, 2 * n + m:2 * n + m + 1], ALU.add,
                                      ALU.mult).then_inc(la_ready, 1)
                for m in range(2):
                    stt(tl(Y, 2 * n + m), ti[m], 1.0, tl(Y, 2 * n + m), ALU.add, ALU.mult).then_inc(la_ready, 1)

            def variances(n):
                la, ti, _ = slots(n)
                dve.wait_ge(lru_exp, 6 * n + 6)
                for m in range(2):
                    stt(la[m], ti[m], 1.0, la[m], ALU.add, ALU.mult).then_inc(var_ready, 1)

            def scans(n):
                la, ti, a = slots(n)
                dve.wait_ge(lru_root, 2 * n + 2)
                dve.wait_ge(la_ready, 4 * n + 4)
                for m in range(2):
                    did(stt(tl(Y, 2 * n + m), la[m], 0.5, tl(Y, 2 * n + m), ALU.mult, ALU.mult))
                for m in range(2):
                    settle(1)
                    did(dve.tensor_tensor_scan(ti[m], a[m], tl(Y, 2 * n + m), 0.0, ALU.mult, ALU.add))
                dve.wait_ge(sg_ready, NT)
                for m in range(2):
                    settle(1 - m)
                    dve.tensor_tensor(tl(Y, 2 * n + m), ti[m], tl(H, 2 * n + m), ALU.mult).then_inc(y2_ready, 1)

            def ylow(n):
                for m in range(2):
                    xlow(2 * n + m, tl(Y, 2 * n + m), xb + 2 * NT + 2 * n + m + 1)

            inputs(0)
            for n in range(8):
                variances(n)
                if n < 7:
                    inputs(n + 1)
                if n:
                    ylow(n - 1)
                scans(n)
            ylow(7)

            did(dve.memset(acc[:, :], 0.0))
            settle()

            def osum(t0, j, i=0):
                dve.wait_ge(osq_ready, i * 2 + (t0 + j + 1))
                dve.tensor_tensor(acc[:, :], acc[:, :], tl(T, j), ALU.add).then_inc(osum_ready, 1)
                dve.wait_ge(osum_ready, i * 2 + (t0 + j + 1))

            with chain.loop(0, NT // 2, 0) as i:
                for j in range(2):
                    dve.wait_ge(w_used, i * 4 + (WO0 + 2 * j + 2))
                    dve.tensor_copy(tl(Y, i * 2 + j), G[j][:, :]).then_inc(tile_out, 1)
                    osum(0, j, i)
            inv_rms(rs[:, :], DEPTH * 3 + 3)
            for c in range(4):
                dve.wait_ge(h_in[c], DEPTH * 16 + 32)
            settle()
            for t in range(NT):
                did(stt(tl(T, 2 + t % 2), tl(Y, t), v2[:, W_POST + t:W_POST + t + 1], rs[:, :], ALU.mult, ALU.mult))
                if t:
                    xlow(t - 1, tl(H, t - 1), xb + 3 * NT + t)
                settle()
                dve.tensor_tensor(tl(H, t), tl(H, t), tl(T, 2 + t % 2), ALU.add).then_inc(h2_ready, 1)
            xlow(NT - 1, tl(H, NT - 1), xb + 4 * NT)
            dve.wait_ge(ph_ready, DEPTH + 1)
            dve.tensor_tensor(PL[:, :], praw, PH[:, :].bitcast(F), ALU.subtract).then_inc(pl_ready, 1)

            with chain.loop(0, NT // 2, 0) as i:
                for j in range(2):
                    dve.wait_ge(w_used, i * 4 + (WG0 + 2 * j + 2))
                    dve.tensor_scalar(tl(T, j), G[j][:, :], 0.5, None, ALU.mult).then_inc(tile_out, 1)
                    dve.wait_ge(wg_th, i * 2 + (j + 1))
            for t in range(NT):
                if t % 4 == 0:
                    dve.wait_ge(w_used, WP0 + t // 4 + 1)
                stt(tl(T, t % 4), tl(Y, t), 1.0, SETS[t // 4 % 2][t % 4][:, :], ALU.add, ALU.mult).then_inc(proj_taken, 1)
                if t:
                    dve.wait_ge(proj_taken, t)
                    stt(tl(H, t - 1), tl(T, (t - 1) % 4), 0.5, tl(H, t - 1), ALU.mult, ALU.add).then_inc(o_ready, 1)
            dve.wait_ge(proj_taken, NT)
            stt(tl(H, NT - 1), tl(T, (NT - 1) % 4), 0.5, tl(H, NT - 1), ALU.mult, ALU.add).then_inc(o_ready, 1)

        @block.tensor
        def _(pe):
            def three(bank, s, wt, xh, xl, first, last):
                c = slice(s * UW + wt * P, s * UW + (wt + 1) * P)
                pe.matmul(bank, WH[:, c], xh, start=first, stop=False)
                pe.matmul(bank, WH[:, c], xl, start=False, stop=False)
                return pe.matmul(bank, WL[:, c], xh, start=False, stop=last)

            def unit(u, s, half, bank, x_first=None):
                pe.wait_ge(wl_ready, u + 1)
                for k in range(UT):
                    kt = half * UT + k
                    if x_first is not None:
                        pe.wait_ge(xl_ready, x_first + (kt + 1))
                    last = three(bank[:, :], s, k, tl(XH, kt), tl(XL, kt), kt == 0, kt == NT - 1)
                last.then_inc(w_used, 1)

            def tile(n, u, s, bank, x_first=None):
                pe.wait_ge(tile_out, n + 1)
                unit(u, s, 0, bank, x_first)
                unit(u + 1, s + 1, 1, bank, x_first)

            def two_tiles(n, u, x_first):
                tile(n, u, 0, G[0], x_first)
                tile(n + 1, u + 2, 2, G[1])

            def tiles(n, u, x_first, count, lo=0):
                with pe.Fori(lo, count // 2) as i:
                    two_tiles(n + i * 2, u + i * 4, x_first)

            def stat():
                pe.matmul(N[:, :], ones[:, :], acc[:, :], start=True, stop=True).then_inc(stat_done, 1)

            pe.wait_ge(relb_in, 48)
            pe.matmul(SC[0][0:HQ, :], ones[0:32, 0:HQ], T[0:32, 0:S], start=True, stop=True).then_inc(line_mm, 1)
            pe.wait_ge(init_done, 1)
            pe.wait_ge(const_in, 32)

            with pe.Fori(0, DEPTH) as ly:
                u0 = ly * LAYER_U
                n0 = ly * LAYER_N
                x0 = ly * (3 * NT)
                pe.wait_ge(hsum_ready, ly * NT + NT)
                stat()
                with pe.Fori(0, CT // 2) as i:
                    for k in range(6):
                        tile(n0 + (i * 6 + k), u0 + (i * 12 + 2 * k), 2 * k % RING, G[k % 2], x0 if k == 0 else None)
                for k in range(4):
                    tile(n0 + (N_KV + k), u0 + (KV0 + 2 * k), 2 * k % RING, G[k % 2])
                    if k == 1:
                        pe.wait_ge(ysum_ready, ly * CT + CT)
                        stat()
                pe.wait_ge(vsum_ready, ly * CT + CT)
                stat()
                pe.wait_ge(tile_out, n0 + (N_Z + 2))
                for j in range(2):
                    for t in range(NB):
                        c = slice(t * P, (t + 1) * P)
                        last = pe.transpose(TR[j][:, c], tl(H, PT + j)[:, c], ident[:, :])
                    last.then_inc(vtr_done, 1)

                def pbuf(n):
                    return H[:, AR * S:AR * S + 6 * BLK] if n % 3 == 2 else a2[:, n % 3 * 6 * BLK:(n % 3 + 1) * 6 * BLK]

                def scores(n):
                    kv, b, pr, r0, kvp, lo, nk = pair_of(n)
                    if n:
                        pe.wait_ge(scores_taken, ly * (2 * PAIRS) + 2 * n)
                    for hh in range(2):
                        q = tl(H, QT + 4 * kvp + 2 * pr + hh)
                        pe.matmul(SC[hh][:, 0:nk * BLK], q[r0:r0 + DH, b * BLK:(b + 1) * BLK],
                                  tl(H, KT + kvp)[r0:r0 + DH, lo * BLK:(lo + nk) * BLK],
                                  start=True, stop=True).then_inc(scores_done, 1)

                def turn(n):
                    nk = pair_of(n)[6]
                    pe.wait_ge(probs_ready, ly * (2 * PAIRS) + (2 * n + 2))
                    if n == 0:
                        pe.wait_ge(v_ready, ly * 2 + 2)
                    else:
                        pe.wait_ge(pt_ready, ly * (2 * PAIRS) + 2 * n)
                    for hh in range(2):
                        for k in range(nk):
                            c = slice(k * BLK, (k + 1) * BLK)
                            last = pe.transpose(TR[hh][:, c], pbuf(n)[:, (3 * hh + k) * BLK:(3 * hh + k + 1) * BLK], ident[:, :])
                        last.then_inc(tr_done, 1)

                def values(n):
                    kv, b, pr, r0, kvp, lo, nk = pair_of(n)
                    pe.wait_ge(pt_ready, ly * (2 * PAIRS) + (2 * n + 2))
                    if n:
                        pe.wait_ge(att_ready, ly * PAIRS + n)
                    for k in range(nk):
                        v = H[:, VT * S + (lo + k) * 2 * P + kv * DH:VT * S + (lo + k) * 2 * P + (kv + 1) * DH]
                        last = pe.matmul(VB[r0:r0 + DH, 0:2 * BLK], v,
                                         H[:, PT * S + 2 * k * BLK:PT * S + 2 * (k + 1) * BLK],
                                         start=(k == 0), stop=(k == nk - 1))
                    last.then_inc(pv_done, 1)

                for n in range(PAIRS + 3):
                    if n < PAIRS:
                        if n % 2 == 0:
                            pe.wait_ge(tile_out, n0 + (N_Z + n // 2 + 1))
                        unit(u0 + (Z0 + n), n % RING, n % 2, G[n // 2 % 2])
                        scores(n)
                    if n >= 3:
                        values(n - 3)
                    if 2 <= n < PAIRS + 2:
                        turn(n - 2)

                tiles(n0 + N_OUT, u0 + OUT0, x0 + NT, NT)

                pe.wait_ge(pl_ready, ly + 1)
                for j in range(4):
                    if j == 0:
                        pe.wait_ge(tile_out, n0 + (N_PG + 2))
                    if j >= 2:
                        pe.wait_ge(e_out, ly * NT + 4 * (j - 1))
                    pe.wait_ge(wl_ready, u0 + (PE0 + j + 1))
                    for c in range(4):
                        for k in range(PK):
                            last = three(SETS[j % 2][c][:, :], j, PK * c + k, tl(PH, k), tl(PL, k), k == 0, k == PK - 1)
                    last.then_inc(w_used, 1)
                pe.wait_ge(e_out, ly * NT + 12)
                two_tiles(n0 + N_PG, u0 + PG0, x0 + 2 * NT)
                pe.wait_ge(esum_ready, ly * NT + NT)
                stat()
                tiles(n0 + N_PG, u0 + PG0, x0 + 2 * NT, NT, 1)

            xb = DEPTH * 3 * NT
            pe.wait_ge(hsum_ready, DEPTH * NT + NT)
            stat()
            two_tiles(NB0, XB0, xb)
            pe.wait_ge(xsum_ready, NT)
            stat()
            tiles(NB0, XB0, xb, NT, 1)
            tiles(NB0 + 16, GT0, xb, NT)
            for n in range(8):
                if n == 0:
                    pe.wait_ge(tile_out, NB0 + 32 + 2)
                if n >= 2:
                    pe.wait_ge(ri_taken, 4 * (n - 1))
                pe.wait_ge(wl_ready, RI0 + n + 1)
                pe.wait_ge(xl_ready, xb + NT + 2 * n + 2)
                for c in range(4):
                    for k in range(2):
                        last = three(SETS[n % 2][c][:, :], n % RING, 2 * c + k, tl(XH, 2 * n + k), tl(XL, 2 * n + k),
                                     k == 0, k == 1)
                last.then_inc(w_used, 1)
            pe.wait_ge(ri_taken, 32)
            tiles(NB0 + 32, WO0, xb + 2 * NT, NT)
            pe.wait_ge(osum_ready, NT)
            stat()
            tiles(NB0 + 48, WG0, xb + 3 * NT, NT)
            pe.wait_ge(pl_ready, DEPTH + 1)
            for j in range(4):
                if j == 0:
                    pe.wait_ge(tile_out, NB0 + 64 + 2)
                if j >= 2:
                    pe.wait_ge(proj_taken, 4 * (j - 1))
                pe.wait_ge(wl_ready, WP0 + j + 1)
                for c in range(4):
                    for k in range(PK):
                        last = three(SETS[j % 2][c][:, :], j, PK * c + k, tl(PH, k), tl(PL, k), k == 0, k == PK - 1)
                last.then_inc(w_used, 1)


def units_of(a):
    k, n = a.shape
    return a.reshape(k // P, P, n // P, P).transpose(2, 1, 0, 3).reshape(n // P, P, 2, UW).transpose(0, 2, 1, 3).reshape(-1, P, UW)


def embed_units(a):
    return a.reshape(PK, P, 4, 4, P).transpose(2, 1, 3, 0, 4).reshape(4, P, UW)


def gate_units(r, i):
    import numpy as np
    both = np.stack([r, i], 1)
    return both.reshape(8, 2, 2, P, 2, P).transpose(0, 3, 1, 4, 2, 5).reshape(8, P, UW)


def heads(a, axis):
    import numpy as np
    shape = list(a.shape)
    b = np.moveaxis(a, axis, 0).reshape(2, 2, GQ, DH, -1).swapaxes(1, 2).reshape(shape[axis], -1)
    return np.moveaxis(b.reshape([shape[axis]] + shape[:axis] + shape[axis + 1:]), 0, axis)


def columns(a):
    return a.reshape(-1, P).T


def wide(a):
    return a.T.reshape(-1, P, a.shape[0]).transpose(1, 0, 2).reshape(P, -1)


def distance_tables():
    import numpy as np
    buckets, far = 32, 128
    rel = np.arange(-2 * BLK + 1, 2 * BLK)
    half = buckets // 2
    n = np.abs(rel)
    exact = half // 2
    large = exact + (np.log(np.maximum(n, 1) / exact) / np.log(far / exact) * (half - exact)).astype(np.int32)
    bucket = (rel > 0) * half + np.where(n < exact, n, np.minimum(large, half - 1))
    inside = n <= BLK
    onehot = np.zeros((buckets, S), np.float32)
    onehot[bucket[inside], np.nonzero(inside)[0]] = 1.0
    band = np.full((HQ, S), NEG, np.float32)
    band[:, np.nonzero(inside)[0]] = 0.0
    return onehot, band


def kernel(**inputs):
    import numpy as np
    import concourse.bacc as bacc
    from concourse.bass_utils import run_bass_kernel_spmd as run

    a = {k: np.asarray(v) for k, v in inputs.items()}
    stream, vectors = [], []
    for l in range(DEPTH):
        wi = a["w_in"][l]
        val, glu, az, q, k, v, bz = np.split(wi, np.cumsum([WC, WC, WC, WC, HKV * DH, HKV * DH]), axis=1)
        q, bz = heads(q, 1), heads(bz, 1)
        inter = np.stack([m.reshape(D, CT, P) for m in (glu, val, q)], 2).reshape(D, -1)
        stream.append(units_of(np.concatenate([inter, k, v, az, bz], 1)))
        wo = a["w_out"][l]
        stream.append(units_of(np.concatenate([wo[:WC], heads(wo[WC:], 0)], 0)))
        stream.append(embed_units(a["w_pe"][l]))
        stream.append(units_of(a["w_pg"][l]))
        vectors.append(np.concatenate(
            [columns(a["norm_g"][l]), columns(a["pe_g"][l]), columns(a["conv_b"][l]), columns(a["cln_g"][l]),
             columns(a["cln_b"][l]), np.broadcast_to(a["sink"][l], (P, HQ)),
             a["conv_w"][l].T.reshape(CT, P, TAPS).transpose(1, 0, 2).reshape(P, -1)], 1))
    stream.append(units_of(a["a_w_in_2"][0]))
    stream.append(gate_units(a["a_w_r_2"][0], a["a_w_i_2"][0]))
    stream.append(units_of(a["a_w_out_2"][0]))
    stream.append(units_of(a["ple_w_gate_2"][0]))
    stream.append(embed_units(a["ple_w_proj_2"][0]))
    vec2 = np.concatenate(
        [columns(a[n].reshape(-1)) for n in ("final_g", "norm_pre_2", "norm_post_2", "a_conv_b_2", "a_b_r_2",
                                             "a_b_i_2", "a_lam_2")]
        + [a["a_conv_w_2"][0].T.reshape(NT, P, TAPS2).transpose(1, 0, 2).reshape(P, -1)], 1)
    onehot, band = distance_tables()
    arrays = {
        "x": wide(a["x"][0]),
        "pin": np.stack([wide(a["p"][0, 0]), wide(a["p"][1, 0]), wide(a["p_2"][0, 0])]),
        "lvec": np.stack(vectors), "vec2": vec2, "relb": a["rel_bias"], "onehot": onehot, "band": band,
        "ident": np.eye(P, dtype=np.float32), "w": np.concatenate(stream, 0),
    }
    arrays = {k: np.ascontiguousarray(v, np.float32) for k, v in arrays.items()}

    nc = bacc.Bacc("TRN2", target_bir_lowering=False, num_devices=1)
    args = [nc.dram_tensor(f"in_{k}", v.shape, mybir.dt.float32, kind="ExternalInput").ap() for k, v in arrays.items()]
    out = nc.dram_tensor("out", (P, NT * S), mybir.dt.float32, kind="ExternalOutput").ap()
    build(nc, *args, out)
    r = run(nc, [{f"in_{k}": v for k, v in arrays.items()}], core_ids=[0])
    y = r.results[0]["out"]
    return y.reshape(P, NT, S).transpose(1, 0, 2).reshape(D, S).T.reshape(1, S, D)
```

```python
import concourse.bass as bass
from concourse import mybir
from contextlib import ExitStack, contextmanager

D = 2048
S = 512
P = 128
NT = D // P
DEPTH = 2
WC = D // 2
CT = WC // P
DH = 64
HQ, HKV, GQ = 16, 4, 4
TAPS = 31
MID = TAPS // 2
BLK = 128
NB = S // BLK
PK = 2
TAPS2 = 4
EPS = 1e-6
NEG = -1e30
LRU_C = 8.0

UT = 8
UW = UT * P
RING = 4

A_U, KV_U, Z_U, OUT_U, PE_U, PG_U = 48, 8, 32, 32, 4, 32
A0 = 0
KV0 = A0 + A_U
Z0 = KV0 + KV_U
OUT0 = Z0 + Z_U
PE0 = OUT0 + OUT_U
PG0 = PE0 + PE_U
LAYER_U = PG0 + PG_U
GROUPS = 8
GROUP_U = 5
B0 = DEPTH * LAYER_U
XB0 = B0
RG0 = XB0 + 32
WO0 = RG0 + GROUPS * GROUP_U
WP0 = WO0 + 32
WG0 = WP0 + 4
UNITS = WG0 + 32

N_KV, N_Z, N_OUT, N_PG, LAYER_N = 24, 28, 44, 60, 76
NB0 = DEPTH * LAYER_N
PAIRS = HQ // 2 * NB
Z_STEPS = PAIRS + 4
Z_CUTS = [round(s * Z_U * UT / Z_STEPS) for s in range(Z_STEPS + 1)]
UNIT_AT = [next((u for u in range(Z_U) if Z_CUTS[s] <= u * UT + UT - 1 < Z_CUTS[s + 1]), None) for s in range(Z_STEPS)]

V_PEG, V_CB, V_LG, V_LB, V_SINK, V_CW = 0, 16, 24, 32, 40, 56
LV_W = V_CW + CT * TAPS
W_FG, W_PRE, W_POST, W_CB, W_BR, W_BI, W_LAM, W_CW = (16 * i for i in range(8))
W_NORM = W_CW + NT * TAPS2
V2_W = W_NORM + (DEPTH + 1) * NT

A_STEPS = TAPS + 3
LAYER_STEPS = CT * A_STEPS + 200


class Steps:

    def __init__(self, eng, sem):
        self.eng, self.sem, self.base, self.n = eng, sem, 0, 0

    def did(self, ins):
        ins.then_inc(self.sem, 1)
        self.n += 1

    def settle(self, back=0):
        self.eng.wait_ge(self.sem, self.base + (self.n - back))

    @contextmanager
    def loop(self, lo, hi, per):
        base, n = self.base, self.n
        with self.eng.Fori(lo, hi) as i:
            self.base, self.n = base + (i * per + (n - lo * per) if per else n), 0
            yield i
            assert self.n == per, (self.n, per)
        self.base, self.n = base, n + per * (hi - lo)


def pair_of(n):
    t, b = n // NB, n % NB
    lo, hi = max(0, b - 1), min(NB, b + 2)
    return t, b, t // GQ, lo, hi - lo


def build(nc, x, pin, lvec, vec2, relb, onehot, band, eye, w, out):
    F, R32 = mybir.dt.float32, mybir.dt.float32r
    ACT, ALU = mybir.ActivationFunctionType, mybir.AluOpType

    ctx = ExitStack()
    with ctx:
        def sb(name, cols, dt=F):
            return ctx.enter_context(nc.sbuf_tensor(name, [P, cols], dt))

        def sem(name):
            return ctx.enter_context(nc.semaphore(name))

        def tl(buf, t):
            return buf[:, bass.ds(t * S, S)]

        H = sb("H", NT * S)
        AR = 0
        PT = 2
        VT, KT, QT = 4, 6, 8
        XC = 8
        XH = sb("XH", NT * S, R32)
        XL = sb("XL", NT * S, R32)
        raw = sb("raw", RING * UW)
        WH = sb("WH", RING * UW, R32)
        WL = sb("WL", RING * UW, R32)
        Y = sb("Y", NT * S)
        a2 = sb("a2", 6 * S)
        T = sb("T", 6 * S)
        acc = sb("acc", S)
        rs = sb("rs", S)
        ident = sb("ident", P)
        ones = sb("ones", P)
        lv = sb("lv", LV_W)
        v2 = sb("v2", V2_W)
        der = sb("der", 3 * NT)
        sm = sb("sm", 3 * 12)
        eps = sb("eps", 1)

        praw = a2[:, 0:PK * S]
        XCH, XCL = (nc.alloc_sbuf_tensor_at(n, [P, 2 * S], R32, offset=nc.lookup_mloc(H).addr + (XC + 2 * i) * S * 4)
                    for i, n in enumerate(("XCH", "XCL")))
        PH, PL = (nc.alloc_sbuf_tensor_at(n, [P, PK * S], R32, offset=nc.lookup_mloc(a2).addr + (1 + i) * PK * S * 4)
                  for i, n in enumerate(("PH", "PL")))

        banks = [ctx.enter_context(nc.psum_tensor(n, [P, S], F))
                 for n in ("acc0", "acc1", "att", "stat", "sc0", "sc1", "tr0", "tr1")]
        G, VB, N, SC, TR = banks[0:2], banks[2], banks[3], banks[4:6], banks[6:8]
        FOUR = banks[4:8]

        def pbuf(n):
            return H[:, AR * S:AR * S + 6 * BLK] if n % 3 == 2 else a2[:, n % 3 * 6 * BLK:(n % 3 + 1) * 6 * BLK]

        h_spill = nc.dram_tensor("h_spill", [P, NT * S], F).ap()
        line_dram = nc.dram_tensor("bias_line", [HQ, S], F)
        bias_dram = nc.dram_tensor("bias_band", [HQ, P, 3 * BLK], F).ap()

        raw_in = [sem(f"raw_in{s}") for s in range(RING)]
        wh_ready = sem("wh_ready")
        wl_ready = sem("wl_ready")
        w_used = sem("w_used")
        h_in = [sem(f"h_in{c}") for c in range(4)]
        h_out = [sem(f"h_out{c}") for c in range(4)]
        vec2_in = sem("vec2_in")
        ident_in = sem("ident_in")
        relb_in = sem("relb_in")
        lv_in = sem("lv_in")
        line_out = sem("line_out")
        bias_in = sem("bias_in")
        p_in = sem("p_in")
        out_sent = sem("out_sent")
        tile_out = sem("tile_out")
        h_ready = sem("h_ready")
        hsq_ready = sem("hsq_ready")
        hsum_ready = sem("hsum_ready")
        y_ready = sem("y_ready")
        xh_ready = sem("xh_ready")
        xl_ready = sem("xl_ready")
        stat_done = sem("stat_done")
        root_ready = sem("root_ready")
        ones_ready = sem("ones_ready")
        fsq_ready = sem("fsq_ready")
        fsum_ready = sem("fsum_ready")
        norm_ready = sem("norm_ready")
        line_mm = sem("line_mm")
        line_ready = sem("line_ready")
        lam_exp = sem("lam_exp")
        lam_ready = sem("lam_ready")
        glu_th = sem("glu_th")
        ysum_ready = sem("ysum_ready")
        yc_ready = sem("yc_ready")
        ysq_ready = sem("ysq_ready")
        vsum_ready = sem("vsum_ready")
        ln_ready = sem("ln_ready")
        ln_th = sem("ln_th")
        vtr_done = sem("vtr_done")
        v_ready = sem("v_ready")
        z_th = sem("z_th")
        scores_done = sem("scores_done")
        scores_taken = sem("scores_taken")
        shift_ready = sem("shift_ready")
        exp_done = sem("exp_done")
        probs_ready = sem("probs_ready")
        tr_done = sem("tr_done")
        pt_ready = sem("pt_ready")
        pv_done = sem("pv_done")
        att_ready = sem("att_ready")
        ph_ready = sem("ph_ready")
        pl_ready = sem("pl_ready")
        e_done = sem("e_done")
        e_out = sem("e_out")
        esq_ready = sem("esq_ready")
        esum_ready = sem("esum_ready")
        g_th = sem("g_th")
        fvar_ready = sem("fvar_ready")
        xc_ready = sem("xc_ready")
        xch_ready = sem("xch_ready")
        xcl_ready = sem("xcl_ready")
        gt_th = sem("gt_th")
        ri_taken = sem("ri_taken")
        la_ready = sem("la_ready")
        lru_exp = sem("lru_exp")
        var_ready = sem("var_ready")
        lru_root = sem("lru_root")
        y2_ready = sem("y2_ready")
        osq_ready = sem("osq_ready")
        osum_ready = sem("osum_ready")
        ors_ready = sem("ors_ready")
        o_scaled = sem("o_scaled")
        h2_ready = sem("h2_ready")
        wg_th = sem("wg_th")
        o_ready = sem("o_ready")
        dve_chain = sem("dve_chain")

        block = ctx.enter_context(nc.Block())

        @block.sync
        def _(sp):
            def load(v, s):
                sp.dma_start(raw[:, s * UW:(s + 1) * UW],
                             w[bass.ds(v, 1)].rearrange("a p n -> (a p) n")).then_inc(raw_in[s], 16)

            def units(first, lo, hi):
                with sp.Fori(0, (hi - lo) // RING) as i:
                    for s in range(RING):
                        v = first + (i * RING + (lo + s))
                        sp.wait_ge(wl_ready, v + 1)
                        load(v + RING, s)

            def h_dma(c, store):
                part = slice(c * 4 * S, (c + 1) * 4 * S)
                if store:
                    sp.dma_start(h_spill[:, part], H[:, part]).then_inc(h_out[c], 16)
                else:
                    sp.dma_start(H[:, part], h_spill[:, part]).then_inc(h_in[c], 16)

            def load_bias(t):
                c = 3 * S + t % 2 * 6 * BLK
                sp.dma_start(a2[:, c:c + 6 * BLK].rearrange("p (g k) -> p g k", g=2),
                             bias_dram[2 * t:2 * t + 2].rearrange("g q k -> q g k")).then_inc(bias_in, 16)

            def load_x(c):
                sp.dma_start(H[:, c * 4 * S:(c + 1) * 4 * S], x[:, c * 4 * S:(c + 1) * 4 * S]).then_inc(h_in[c], 16)

            load(0, 0)
            sp.dma_start(v2[:, :], vec2).then_inc(vec2_in, 16)
            load_x(0)
            sp.dma_start(ones[0:32, 0:HQ], relb).then_inc(relb_in, 16)
            sp.dma_start(T[0:32, 0:S], onehot).then_inc(relb_in, 16)
            sp.dma_start(T[0:HQ, S:2 * S], band).then_inc(relb_in, 16)
            sp.dma_start(ident[:, :], eye).then_inc(ident_in, 16)
            load_x(1)
            load(1, 1)
            load_x(2)
            load_x(3)
            load(2, 2)
            load(3, 3)
            sp.wait_ge(line_ready, 1)
            sp.dma_start(line_dram.ap(), T[0:HQ, 2 * S:3 * S]).then_inc(line_out, 16)
            for s in range(RING):
                sp.wait_ge(wl_ready, s + 1)
                load(RING + s, s)
                if s < 2:
                    for c in (2 * s, 2 * s + 1):
                        sp.wait_ge(h_in[c], 16)
                        h_dma(c, True)
            sp.wait_ge(line_out, 16)
            sp.dma_start(bias_dram, bass.AP(line_dram, P - 1, [[S, HQ], [-1, P], [1, 3 * BLK]])).then_inc(line_out, 16)

            with sp.Fori(0, DEPTH) as ly:
                u0 = ly * LAYER_U
                sp.wait_ge(hsum_ready, ly * NT + NT)
                sp.dma_start(lv[:, :], lvec[bass.ds(ly, 1)].rearrange("a p n -> (a p) n")).then_inc(lv_in, 16)
                sp.wait_ge(line_out, 32)
                load_bias(0)
                load_bias(1)
                units(u0, 4, Z0 + NB)
                for t in range(2, CT):
                    sp.wait_ge(scores_taken, ly * (2 * PAIRS) + 2 * NB * (t - 1))
                    load_bias(t)
                    units(u0, Z0 + NB * (t - 1), Z0 + NB * t if t < CT - 1 else OUT0)
                sp.wait_ge(y_ready, ly * NT + NT)
                for c in range(4):
                    sp.wait_ge(h_out[c], ly * 16 + 16)
                    h_dma(c, False)
                units(u0, OUT0, OUT0 + 8)
                sp.wait_ge(tr_done, ly * (2 * PAIRS) + 2 * PAIRS)
                sp.dma_start(praw, pin[bass.ds(ly, 1)].rearrange("a p n -> (a p) n")).then_inc(p_in, 16)
                units(u0, OUT0 + 8, PG0 + 12)
                for c in range(4):
                    sp.wait_ge(h_ready, ly * NT + 4 * (c + 1))
                    h_dma(c, True)
                    if c < 3:
                        units(u0, PG0 + 12 + 8 * c, PG0 + 20 + 8 * c)

            units(B0, 4, WO0 - B0)
            sp.wait_ge(y2_ready, NT)
            for c in range(4):
                sp.wait_ge(h_out[c], DEPTH * 16 + 16)
                h_dma(c, False)
            sp.dma_start(praw, pin[DEPTH]).then_inc(p_in, 16)
            units(B0, WO0 - B0, UNITS - B0 - RING)
            for lo, hi in ((0, 4), (4, 8), (8, 12), (12, 14), (14, 16)):
                sp.wait_ge(o_ready, hi)
                sp.dma_start(out[:, lo * S:hi * S], H[:, lo * S:hi * S]).then_inc(out_sent, 16)
            sp.wait_ge(out_sent, 5 * 16)

        @block.gpsimd
        def _(pool):
            def lows(lo, hi):
                with pool.Fori(lo // RING, hi // RING) as i:
                    for s in range(RING):
                        pool.wait_ge(wh_ready, i * RING + (s + 1))
                        c = slice(s * UW, (s + 1) * UW)
                        pool.tensor_tensor(WL[:, c], raw[:, c], WH[:, c].bitcast(F),
                                           ALU.subtract).then_inc(wl_ready, 1)

            lows(0, WP0 + RING)
            pool.wait_ge(ors_ready, 1)
            for t in range(1, NT, 2):
                pool.tensor_tensor(tl(Y, t), tl(Y, t), rs[:, :], ALU.mult).then_inc(o_scaled, 1)
            lows(WP0 + RING, UNITS)

        @block.scalar
        def _(act):
            def high(s):
                c = slice(s * UW, (s + 1) * UW)
                act.activation(WH[:, c], raw[:, c], ACT.Copy).then_inc(wh_ready, 1)

            def prep(first, v):
                act.wait_ge(raw_in[v % RING], first * (16 // RING) + 16 * (v // RING + 2))
                act.wait_ge(w_used, first + (v + 1))
                high(v % RING)

            def prep_loop(first, lo, n, i, per):
                act.wait_ge(raw_in[n % RING], first * (16 // RING) + (i * (16 * per // RING) + 16 * ((lo + n) // RING + 2)))
                act.wait_ge(w_used, first + (i * per + (lo + n + 1)))
                high(n % RING)

            def preps(first, lo, hi):
                with act.Fori(0, (hi - lo) // RING) as i:
                    for s in range(RING):
                        prep_loop(first, lo, s, i, RING)

            def xhigh(t, src, scale=1.0):
                act.activation(tl(XH, t), src, ACT.Copy, scale=scale).then_inc(xh_ready, 1)

            def root(dst, count, mean):
                act.wait_ge(stat_done, count)
                act.activation(dst, N[:, :], ACT.Sqrt, bias=eps[:, 0:1], scale=mean).then_inc(root_ready, 1)

            def norm_col(n, t):
                return v2[:, bass.ds(n * NT + (W_NORM + t), 1)]

            act.wait_ge(vec2_in, 16)
            for t in range(NT):
                if t % 8 == 0:
                    act.wait_ge(raw_in[t // 8], 16)
                    high(t // 8)
                if t % 4 == 0:
                    act.wait_ge(h_in[t // 4], 16)
                xhigh(t, tl(H, t), v2[:, W_NORM + t:W_NORM + t + 1])
            for t in range(NT):
                if t < 2:
                    act.wait_ge(raw_in[2 + t], 16)
                    high(2 + t)
                if t >= 3:
                    act.wait_ge(hsum_ready, t - 2)
                act.activation(tl(T, 3 + t % 3), tl(H, t), ACT.Square).then_inc(hsq_ready, 1)

            act.wait_ge(norm_ready, 1)
            with act.Fori(0, DEPTH) as ly:
                u0 = ly * LAYER_U
                n0 = ly * LAYER_N

                root(rs[:, :], ly * 4 + 1, 1.0 / D)

                with act.Fori(0, CT // 2) as i:
                    for h in range(2):
                        for k in range(6):
                            prep_loop(u0, A0, 6 * h + k, i, 12)
                            if k == 2:
                                act.wait_ge(tile_out, n0 + (i * 6 + (3 * h + 1 + 2)))
                                act.activation(tl(T, h), tl(T, h), ACT.Tanh).then_inc(glu_th, 1)

                prep(u0, KV0)
                prep(u0, KV0 + 1)
                prep(u0, KV0 + 2)
                prep(u0, KV0 + 3)
                for t in range(CT):
                    act.wait_ge(yc_ready, ly * CT + (t + 1))
                    if t >= 2:
                        act.wait_ge(vsum_ready, ly * CT + (t - 1))
                    act.activation(tl(T, t % 2), tl(Y, t), ACT.Square).then_inc(ysq_ready, 1)
                    if t in (3, 7):
                        prep(u0, KV0 + 4 + t // 4)
                prep(u0, KV0 + 6)
                root(tl(T, 4), ly * 4 + 3, 1.0 / WC)
                prep(u0, KV0 + 7)
                for j in range(2):
                    act.wait_ge(vtr_done, ly * 2 + (j + 1))
                    act.activation(H[:, VT * S:(VT + 2) * S].rearrange("p (t c) -> p t c", t=NB)[:, :, j * P:(j + 1) * P],
                                   TR[j][:, :].rearrange("p (t c) -> p t c", t=NB), ACT.Copy).then_inc(v_ready, 1)

                def exps(n):
                    st = sm[:, 12 * (n % 3):12 * (n % 3) + 12]
                    keys = pair_of(n)[4] * BLK
                    act.wait_ge(shift_ready, ly * PAIRS + (n + 1))
                    for hh in range(2):
                        pb = pbuf(n)[:, hh * 3 * BLK:hh * 3 * BLK + keys]
                        act.activation(pb, pb, ACT.Exp, bias=st[:, 2 + hh:3 + hh], accum_out=st[:, 6 + hh:7 + hh])
                    act.activation(st[:, 8:10], st[:, 4:6], ACT.Exp).then_inc(exp_done, 1)

                def probs_out(n):
                    nk = pair_of(n)[4]
                    if n:
                        act.wait_ge(pv_done, ly * PAIRS + n)
                    pt = H[:, PT * S:PT * S + 6 * BLK].rearrange("p (k h q) -> p k h q", k=3, h=2)
                    for hh in range(2):
                        act.wait_ge(tr_done, ly * (2 * PAIRS) + (2 * n + hh + 1))
                        act.activation(pt[:, 0:nk, hh, :], TR[hh][:, 0:nk * BLK].rearrange("p (k q) -> p k q", k=nk),
                                       ACT.Copy).then_inc(pt_ready, 1)

                for n, u in enumerate(UNIT_AT):
                    if u is not None:
                        if u == Z_U - 1:
                            act.wait_ge(w_used, u0 + OUT0)
                            for t in range(2):
                                xhigh(t, tl(Y, t))
                        else:
                            prep(u0, Z0 + u)
                        if u % 2 == 1:
                            j = u // 2
                            act.wait_ge(tile_out, n0 + (N_Z + j + 1 + 2))
                            act.activation(tl(T, 2 + j % 2), tl(T, j % 2), ACT.Tanh).then_inc(z_th, 1)
                    if n < PAIRS:
                        exps(n)
                    if 2 <= n < PAIRS + 2:
                        probs_out(n - 2)
                    if u is not None and u % 2 == 0 and u // 2 < CT:
                        act.wait_ge(ln_ready, ly * CT + (u // 2 + 1))
                        act.activation(tl(T, 5), tl(Y, u // 2), ACT.Tanh).then_inc(ln_th, 1)
                prep(u0, OUT0 - 1)
                for t in range(2, NT):
                    act.wait_ge(y_ready, ly * NT + (t + 1))
                    xhigh(t, tl(Y, t))
                preps(u0, OUT0, OUT0 + 16)
                act.wait_ge(p_in, ly * 16 + 16)
                act.activation(PH[:, :], praw, ACT.Copy).then_inc(ph_ready, 1)
                preps(u0, OUT0 + 16, PE0)

                for t in range(NT):
                    if t % 4 == 3:
                        prep(u0, PE0 + t // 4)
                    else:
                        act.wait_ge(e_done, ly * 12 + (t // 4 * 3 + t % 4 + 1))
                    act.activation(tl(Y, t), FOUR[t % 4][:, :], ACT.Copy, scale=0.5).then_inc(e_out, 1)
                    if t == 0:
                        act.wait_ge(tile_out, n0 + (N_PG + 2))
                    xhigh(t, tl(H, t))
                for t in range(NT):
                    if t % 8 == 0:
                        prep(u0, PG0 + t // 8)
                    if t == 0:
                        act.wait_ge(e_out, ly * NT + NT)
                    if t >= 2:
                        act.wait_ge(esum_ready, ly * NT + (t - 1))
                    act.activation(tl(T, 2 + t % 2), tl(Y, t), ACT.Square).then_inc(esq_ready, 1)
                prep(u0, PG0 + 2)
                prep(u0, PG0 + 3)
                root(rs[:, :], ly * 4 + 4, 4.0 / D)

                def gate(first, j, slot, i=0):
                    act.wait_ge(tile_out, n0 + (i * 2 + (N_PG + first + j + 1 + 2)))
                    act.activation(tl(T, slot), tl(T, slot), ACT.Tanh).then_inc(g_th, 1)

                def square(first, j, i=0):
                    t = i * 2 + (first + j)
                    act.wait_ge(h_ready, ly * NT + (i * 2 + (first + j + 1)))
                    act.activation(tl(T, 2 + (first + j) % 2), tl(H, t), ACT.Square).then_inc(hsq_ready, 1)
                    act.wait_ge(fsum_ready, ly * (NT + 1) + (i * 2 + (first + j + 1)))
                    act.activation(tl(T, 5), tl(H, t), ACT.Square,
                                   scale=v2[:, bass.ds(t + W_FG, 1)]).then_inc(fsq_ready, 1)

                gate(0, 0, 0)
                gate(0, 1, 1)
                square(0, 0)
                with act.Fori(0, NT // 2 - 1) as i:
                    for j in range(2):
                        prep_loop(u0, PG0 + 4, 2 * j, i, 4)
                        act.wait_ge(hsum_ready, ly * NT + (i * 2 + (NT + j)))
                        square(1, j, i)
                        gate(2, j, j, i)
                        prep_loop(u0, PG0 + 4, 2 * j + 1, i, 4)
                for t in range(NT):
                    if t == NT - 1:
                        act.wait_ge(h_ready, ly * NT + NT)
                    xhigh(t, tl(H, t), norm_col(ly + 1, t))
                act.wait_ge(hsum_ready, ly * NT + (2 * NT - 2))
                square(NT - 1, 0)

            act.wait_ge(fsum_ready, DEPTH * (NT + 1))
            prep(B0, 0)
            root(tl(T, 5), DEPTH * 4 + 1, 1.0 / D)
            prep(B0, 1)
            act.wait_ge(fvar_ready, 1)
            act.activation(rs[:, :], tl(T, 4), ACT.Sqrt, bias=eps[:, 0:1], scale=1.0 / D).then_inc(root_ready, 1)
            prep(B0, 2)
            prep(B0, 3)
            preps(B0, 4, 16)
            act.wait_ge(lam_ready, 1)
            act.activation(T[:, 4 * S:4 * S + NT], T[:, 4 * S:4 * S + NT], ACT.Exp, scale=-1.0).then_inc(lam_exp, 1)
            preps(B0, 16, RG0 - B0)

            la, ti, dk = (lambda m: tl(a2, m)), (lambda m: tl(a2, 2 + m)), (lambda m: tl(a2, 4 + m))

            for c in range(4):
                act.wait_ge(h_out[c], DEPTH * 16 + 16)
            with act.Fori(0, GROUPS // RING) as r:
                for g in range(RING):
                    k = GROUP_U * g
                    ready = lambda n: prep_loop(B0, RG0 - B0, k + n, r, RING * GROUP_U)

                    def gate_tanh(m):
                        act.wait_ge(tile_out, r * (2 * RING) + (NB0 + 16 + 2 * g + m + 1 + 2))
                        act.activation(tl(T, 2 + m), tl(T, m), ACT.Tanh).then_inc(gt_th, 1)

                    for m in range(2):
                        act.wait_ge(xc_ready, r * (2 * RING) + (2 * g + m + 1))
                        act.activation(tl(XCH, m), tl(Y, r * (2 * RING) + (2 * g + m)), ACT.Copy).then_inc(xch_ready, 1)
                    ready(0)
                    act.wait_ge(w_used, r * (GROUP_U * RING) + (RG0 + k + 2))
                    act.wait_ge(xcl_ready, r * (2 * RING) + (2 * g + 2))
                    for q, dst in ((0, la), (1, ti)):
                        for m in range(2):
                            half_bias = der[:, bass.ds(r * (2 * RING) + ((1 + q) * NT + 2 * g + m), 1)]
                            act.activation(dst(m), FOUR[2 * q + m][:, :], ACT.Tanh, scale=0.5,
                                           bias=half_bias).then_inc(ri_taken, 1)
                    ready(1)
                    act.wait_ge(la_ready, r * (4 * RING) + (4 * g + 4))
                    for m in range(2):
                        act.activation(dk(m), la(m), ACT.Exp).then_inc(lru_exp, 1)
                    for m in range(2):
                        act.activation(la(m), la(m), ACT.Tanh, scale=-1.0).then_inc(lru_exp, 1)
                    act.wait_ge(lru_exp, r * (6 * RING) + (6 * g + 2))
                    for m in range(2):
                        act.activation(ti(m), dk(m), ACT.Square).then_inc(lru_exp, 1)
                    ready(2)
                    gate_tanh(0)
                    act.wait_ge(var_ready, r * (2 * RING) + (2 * g + 2))
                    for m in range(2):
                        act.activation(la(m), la(m), ACT.Sqrt).then_inc(lru_root, 1)
                    ready(3)
                    gate_tanh(1)
                    ready(4)
            act.wait_ge(w_used, WO0)
            for t in range(NT):
                act.wait_ge(y2_ready, t + 1)
                xhigh(t, tl(Y, t))

            def osquares(lo, hi):
                with act.Fori(lo, hi) as i:
                    for j in range(2):
                        prep_loop(B0, WO0 - B0, 2 * j, i, 4)
                        prep_loop(B0, WO0 - B0, 2 * j + 1, i, 4)
                        act.wait_ge(tile_out, i * 2 + (NB0 + 32 + j + 1))
                        act.activation(tl(T, j), G[j][:, :], ACT.Square).then_inc(osq_ready, 1)

            osquares(0, 4)
            act.wait_ge(p_in, DEPTH * 16 + 16)
            act.activation(PH[:, :], praw, ACT.Copy).then_inc(ph_ready, 1)
            osquares(4, 8)
            root(rs[:, :], DEPTH * 4 + 3, 1.0 / D)
            for t in range(NT):
                if t % 4 == 3:
                    prep(B0, WP0 - B0 + t // 4)
                else:
                    act.wait_ge(e_done, DEPTH * 12 + (t // 4 * 3 + t % 4 + 1))
                if t >= 4:
                    act.wait_ge(h2_ready, t - 3)
                act.activation(tl(T, 2 + t) if t < 4 else tl(Y, t - 4), FOUR[t % 4][:, :], ACT.Copy,
                               scale=0.5).then_inc(e_out, 1)
                if t >= 4:
                    xhigh(t - 4, tl(H, t - 4))
            for t in range(NT - 4, NT):
                act.wait_ge(h2_ready, t + 1)
                xhigh(t, tl(H, t))

            def wgate(first, j, i=0):
                act.wait_ge(tile_out, i * 2 + (NB0 + 48 + first + j + 1 + 2))
                act.activation(tl(T, j), tl(T, j), ACT.Tanh).then_inc(wg_th, 1)

            with act.Fori(0, NT // 2 - 1) as i:
                for j in range(2):
                    prep_loop(B0, WG0 - B0, 2 * j, i, 4)
                    prep_loop(B0, WG0 - B0, 2 * j + 1, i, 4)
                    wgate(0, j, i)
            for j in range(2):
                wgate(NT - 2, j)

        @block.vector
        def _(dve):
            chain = Steps(dve, dve_chain)
            did, settle = chain.did, chain.settle

            def col(v, c):
                return v[:, bass.ds(c, 1)]

            def stt(out_, in0, scalar, in1, op0, op1):
                return dve.scalar_tensor_tensor(out_, in0, scalar, in1, op0, op1)

            def xlow(t, src, count, scale=1.0):
                dve.wait_ge(xh_ready, count)
                stt(tl(XL, t), src, scale, tl(XH, t).bitcast(F), ALU.mult, ALU.subtract).then_inc(xl_ready, 1)

            def inv_rms(dst, count):
                dve.wait_ge(root_ready, count)
                did(dve.reciprocal(dst, dst))

            dve.memset(eps[:, :], EPS).then_inc(tile_out, 1)
            did(dve.memset(rs[:, :], 0.0))
            dve.memset(acc[:, :], 0.0).then_inc(tile_out, 1)
            dve.wait_ge(vec2_in, 16)
            pre2 = v2[:, W_NORM + DEPTH * NT:W_NORM + (DEPTH + 1) * NT]
            dve.tensor_tensor(pre2, pre2, v2[:, W_PRE:W_PRE + NT], ALU.mult).then_inc(norm_ready, 1)
            dve.wait_ge(tile_out, 2)
            for t in range(NT):
                xlow(t, tl(H, t), t + 1, v2[:, W_NORM + t:W_NORM + t + 1])
                if t == 3:
                    dve.wait_ge(line_mm, 1)
                    dve.tensor_tensor(T[0:HQ, 2 * S:3 * S], SC[0][0:HQ, :], T[0:HQ, S:2 * S], ALU.add).then_inc(line_ready, 1)
                    dve.memset(ones[:, :], 1.0).then_inc(ones_ready, 1)
            for t in range(NT):
                part = acc if t % 2 == 0 else rs
                dve.wait_ge(hsq_ready, t + 1)
                if t >= 2:
                    dve.wait_ge(hsum_ready, t - 1)
                add = dve.tensor_tensor(part[:, :], part[:, :], tl(T, 3 + t % 3), ALU.add)
                if t < NT - 1:
                    add.then_inc(hsum_ready, 1)
                else:
                    did(add)
            settle()
            dve.wait_ge(hsum_ready, NT - 1)
            dve.tensor_tensor(acc[:, :], acc[:, :], rs[:, :], ALU.add).then_inc(hsum_ready, 1)
            dve.wait_ge(norm_ready, 1)

            with chain.loop(0, DEPTH, LAYER_STEPS) as ly:
                u0 = ly * LAYER_U
                n0 = ly * LAYER_N
                x0 = ly * (3 * NT)

                def taken(n):
                    dve.wait_ge(w_used, u0 + n)

                inv_rms(rs[:, :], ly * 3 + 1)
                settle()
                for c in range(4):
                    dve.wait_ge(h_out[c], ly * 16 + 16)
                did(dve.memset(acc[:, :], 0.0))

                with chain.loop(0, CT // 2, 2 * A_STEPS) as i:
                    for h in range(2):
                        t = i * 2 + h
                        u = i * 12 + 6 * h
                        n = i * 6 + 3 * h
                        a = tl(H, AR + h)
                        y = tl(Y, t)
                        taken(u + 2)
                        stt(tl(T, h), G[h % 2][:, :], 0.5, rs[:, :], ALU.mult, ALU.mult).then_inc(tile_out, 1)
                        taken(u + 4)
                        stt(tl(T, 2), G[(h + 1) % 2][:, :], 0.5, rs[:, :], ALU.mult, ALU.mult).then_inc(tile_out, 1)
                        dve.wait_ge(glu_th, ly * CT + (t + 1))
                        dve.wait_ge(tile_out, n0 + (n + 2 + 2))
                        did(stt(a, tl(T, h), 1.0, tl(T, 2), ALU.add, ALU.mult))
                        settle()
                        dve.wait_ge(lv_in, ly * 16 + 16)
                        wcol = lambda j: col(lv, t * TAPS + (V_CW + j))
                        did(dve.tensor_scalar(y, a, wcol(MID), col(lv, t + V_CB), ALU.mult, ALU.add))
                        c2 = tl(T, 3)
                        did(dve.memset(c2, 0.0))
                        side = [j for j in range(TAPS) if j != MID]
                        for k, j in enumerate(side):
                            lo, hi = max(0, MID - j), min(S, S + MID - j)
                            dst = y if k % 2 == 0 else c2
                            settle(1)
                            did(stt(dst[:, lo:hi], a[:, lo + j - MID:hi + j - MID], wcol(j), dst[:, lo:hi],
                                    ALU.mult, ALU.add))
                            if k == 18:
                                taken(u + 6)
                                stt(tl(H, t + QT), G[h % 2][:, :], DH ** -0.5, rs[:, :],
                                    ALU.mult, ALU.mult).then_inc(tile_out, 1)
                        settle()
                        did(dve.tensor_tensor(y, y, c2, ALU.add))
                        settle()
                        dve.tensor_tensor(acc[:, :], acc[:, :], y, ALU.add).then_inc(ysum_ready, 1)
                        dve.wait_ge(ysum_ready, ly * CT + (t + 1))

                for j in range(2):
                    taken(KV0 + 2 * j + 2)
                    dve.tensor_tensor(tl(H, KT + j), G[j][:, :], rs[:, :], ALU.mult).then_inc(tile_out, 1)
                dve.wait_ge(stat_done, ly * 4 + 2)
                did(dve.tensor_scalar(tl(T, 4), N[:, :], 1.0 / WC, None, ALU.mult))
                did(dve.memset(acc[:, :], 0.0))
                settle()
                for t in range(CT):
                    dve.tensor_tensor(tl(Y, t), tl(Y, t), tl(T, 4), ALU.subtract).then_inc(yc_ready, 1)

                def vsum(t):
                    dve.wait_ge(ysq_ready, ly * CT + (t + 1))
                    if t:
                        dve.wait_ge(vsum_ready, ly * CT + t)
                    dve.tensor_tensor(acc[:, :], acc[:, :], tl(T, t % 2), ALU.add).then_inc(vsum_ready, 1)

                for t in range(CT):
                    vsum(t)

                def values(j):
                    taken(KV0 + 4 + 2 * j + 2)
                    dve.tensor_tensor(tl(H, PT + j), G[j][:, :], rs[:, :], ALU.mult).then_inc(tile_out, 1)

                values(0)
                inv_rms(tl(T, 4), ly * 3 + 2)
                values(1)

                def ln(t):
                    settle()
                    did(stt(tl(Y, t), tl(Y, t), lv[:, V_LG + t:V_LG + t + 1], tl(T, 4), ALU.mult, ALU.mult))
                    settle()
                    dve.tensor_scalar(tl(Y, t), tl(Y, t), lv[:, V_LB + t:V_LB + t + 1], 0.5, ALU.add,
                                      ALU.mult).then_inc(ln_ready, 1)

                def swish(t):
                    dve.wait_ge(ln_th, ly * CT + (t + 1))
                    did(stt(tl(Y, t), tl(T, 5), 1.0, tl(Y, t), ALU.add, ALU.mult))

                def stats(n):
                    return sm[:, 12 * (n % 3):12 * (n % 3) + 12]

                def scores(n):
                    t, b, _, lo, nk = pair_of(n)
                    st = stats(n)
                    if b == 0:
                        dve.wait_ge(bias_in, ly * (16 * CT) + 16 * (t + 1))
                    h0 = V_SINK + 2 * t
                    dve.wait_ge(scores_done, ly * (2 * PAIRS) + (2 * n + 2))
                    did(dve.tensor_copy(st[:, 4:6], lv[:, h0:h0 + 2]))
                    for hh in range(2):
                        off = 3 * S + (t % 2 * 2 + hh) * 3 * BLK + (BLK if b == 0 else 0)
                        dve.tensor_tensor_reduce(pbuf(n)[:, hh * 3 * BLK:hh * 3 * BLK + nk * BLK],
                                                 SC[hh][:, 0:nk * BLK], a2[:, off:off + nk * BLK], 1.0,
                                                 lv[:, h0 + hh:h0 + hh + 1],
                                                 ALU.add, ALU.max, st[:, hh:hh + 1]).then_inc(scores_taken, 1)
                    dve.wait_ge(scores_taken, ly * (2 * PAIRS) + (2 * n + 2))
                    did(dve.tensor_scalar(st[:, 2:4], st[:, 0:2], -1.0, None, ALU.mult))
                    dve.tensor_tensor(st[:, 4:6], st[:, 4:6], st[:, 0:2], ALU.subtract).then_inc(shift_ready, 1)

                def finish(n):
                    st = stats(n)
                    keys = pair_of(n)[4] * BLK
                    dve.wait_ge(exp_done, ly * PAIRS + (n + 1))
                    did(dve.tensor_tensor(st[:, 10:12], st[:, 6:8], st[:, 8:10], ALU.add))
                    settle()
                    did(dve.reciprocal(st[:, 10:12], st[:, 10:12]))
                    settle()
                    for hh in range(2):
                        pb = pbuf(n)[:, hh * 3 * BLK:hh * 3 * BLK + keys]
                        ins = dve.tensor_scalar(pb, pb, st[:, 10 + hh:11 + hh], None, ALU.mult)
                        ins.then_inc(probs_ready, 1)

                def att_out(n):
                    t, b, _, _, _ = pair_of(n)
                    dve.wait_ge(pv_done, ly * PAIRS + (n + 1))
                    dve.tensor_copy(tl(H, QT + t)[:, b * BLK:(b + 1) * BLK], VB[:, 0:BLK]).then_inc(att_ready, 1)

                def silu(j):
                    dve.wait_ge(z_th, ly * NT + (j + 1))
                    did(stt(tl(T, j % 2), tl(T, 2 + j % 2), 1.0, tl(T, j % 2), ALU.add, ALU.mult))
                    if j >= CT:
                        dve.wait_ge(att_ready, ly * PAIRS + NB * (j - CT + 1))
                    settle()
                    dve.tensor_tensor(tl(Y, j), tl(Y, j) if j < CT else tl(H, QT + j - CT), tl(T, j % 2),
                                      ALU.mult).then_inc(y_ready, 1)

                for n, u in enumerate(UNIT_AT):
                    if 1 <= n <= PAIRS:
                        finish(n - 1)
                    if n < PAIRS:
                        scores(n)
                    if u is not None and u % 2 == 0:
                        if u >= 2:
                            silu(u // 2 - 1)
                        if u // 2 < CT:
                            ln(u // 2)
                    if u is not None and u % 2 == 1:
                        j = u // 2
                        if j < CT:
                            swish(j)
                        taken(Z0 + 2 * j + 2)
                        stt(tl(T, j % 2), G[j % 2][:, :], 0.5, rs[:, :], ALU.mult, ALU.mult).then_inc(tile_out, 1)
                    if 3 <= n < PAIRS + 3:
                        att_out(n - 3)

                for t in range(NT):
                    if t == 2:
                        silu(NT - 1)
                    xlow(t, tl(Y, t), x0 + (NT + t + 1))

                def add_out(i, j):
                    t = i * 2 + j
                    for c in range(4):
                        dve.wait_ge(h_in[c], ly * 16 + 32)
                    taken(i * 4 + (OUT0 + 2 * j + 2))
                    dve.tensor_tensor(tl(H, t), tl(H, t), G[j][:, :], ALU.add).then_inc(tile_out, 1)

                with chain.loop(0, 4, 0) as i:
                    for j in range(2):
                        add_out(i, j)
                dve.wait_ge(ph_ready, ly + 1)
                dve.tensor_tensor(PL[:, :], praw, PH[:, :].bitcast(F), ALU.subtract).then_inc(pl_ready, 1)
                with chain.loop(4, 8, 0) as i:
                    for j in range(2):
                        add_out(i, j)

                dve.wait_ge(tile_out, n0 + (N_PG + 2))
                for t in range(NT):
                    xlow(t, tl(H, t), x0 + (2 * NT + t + 1))
                did(dve.memset(acc[:, :], 0.0))
                settle()
                for t in range(NT):
                    dve.wait_ge(esq_ready, ly * NT + (t + 1))
                    if t:
                        dve.wait_ge(esum_ready, ly * NT + t)
                    dve.tensor_tensor(acc[:, :], acc[:, :], tl(T, 2 + t % 2), ALU.add).then_inc(esum_ready, 1)

                def halve(t0, j, i=0):
                    taken(i * 4 + (PG0 + 2 * (t0 + j) + 2))
                    dve.tensor_scalar(tl(T, j), G[j][:, :], 0.5, None, ALU.mult).then_inc(tile_out, 1)

                def scaled(t0, j, i=0):
                    t = i * 2 + (t0 + j)
                    did(stt(tl(Y, t), tl(Y, t), col(lv, t + V_PEG), rs[:, :], ALU.mult, ALU.mult))

                def gated(t0, j, i=0):
                    t = i * 2 + (t0 + j)
                    dve.wait_ge(g_th, ly * NT + (i * 2 + (t0 + j + 1)))
                    did(stt(tl(T, j), tl(T, j), 1.0, tl(Y, t), ALU.add, ALU.mult))
                    settle()
                    dve.tensor_tensor(tl(H, t), tl(H, t), tl(T, j), ALU.add).then_inc(h_ready, 1)

                def sums(t0, j, i=0):
                    dve.wait_ge(hsq_ready, ly * NT + (i * 2 + (NT + t0 + j + 1)))
                    dve.wait_ge(hsum_ready, ly * NT + (i * 2 + (NT + t0 + j)))
                    dve.tensor_tensor(acc[:, :], acc[:, :], tl(T, 2 + j), ALU.add).then_inc(hsum_ready, 1)
                    dve.wait_ge(fsq_ready, ly * NT + (i * 2 + (t0 + j + 1)))
                    dve.wait_ge(fsum_ready, ly * (NT + 1) + (i * 2 + (t0 + j + 1)))
                    dve.tensor_tensor(tl(T, 4), tl(T, 4), tl(T, 5), ALU.add).then_inc(fsum_ready, 1)

                halve(0, 0)
                halve(0, 1)
                inv_rms(rs[:, :], ly * 3 + 3)
                did(dve.memset(acc[:, :], 0.0))
                dve.memset(tl(T, 4), 0.0).then_inc(fsum_ready, 1)
                settle()
                scaled(0, 0)
                scaled(0, 1)
                settle()
                gated(0, 0)
                gated(0, 1)
                with chain.loop(0, NT // 2 - 1, 4) as i:
                    for j in range(2):
                        sums(0, j, i)
                        scaled(2, j, i)
                        halve(2, j, i)
                        settle()
                        gated(2, j, i)
                for t in range(NT):
                    xlow(t, tl(H, t), x0 + (3 * NT + t + 1), col(v2, ly * NT + (W_NORM + NT + t)))
                sums(NT - 2, 0)
                sums(NT - 2, 1)

            xb = DEPTH * 3 * NT
            rs1 = tl(T, 5)
            inv_rms(rs1, DEPTH * 3 + 1)
            settle()
            dve.wait_ge(stat_done, DEPTH * 4 + 2)
            did(dve.tensor_tensor(tl(T, 4), VB[:, :], rs1, ALU.mult))
            settle()
            dve.tensor_tensor(tl(T, 4), tl(T, 4), rs1, ALU.mult).then_inc(fvar_ready, 1)
            inv_rms(rs[:, :], DEPTH * 3 + 2)
            settle()
            did(dve.tensor_tensor(rs[:, :], rs[:, :], rs1, ALU.mult))
            settle()

            def conv_loop(lo, hi):
                with chain.loop(lo, hi, 2 * (TAPS2 - 1)) as i:
                    for j in range(2):
                        t = i * 2 + j
                        dve.wait_ge(w_used, i * 4 + (XB0 + 2 * j + 2))
                        dve.tensor_tensor(tl(T, j), G[j][:, :], rs[:, :], ALU.mult).then_inc(tile_out, 1)
                        dve.wait_ge(tile_out, i * 2 + (NB0 + j + 1 + 2))
                        y = tl(Y, t)
                        did(dve.tensor_scalar(y, tl(T, j), col(v2, t * TAPS2 + (W_CW + TAPS2 - 1)), col(v2, t + W_CB),
                                              ALU.mult, ALU.add))
                        for k in range(TAPS2 - 2, -1, -1):
                            back = TAPS2 - 1 - k
                            settle()
                            ins = stt(y[:, back:S], tl(T, j)[:, 0:S - back], col(v2, t * TAPS2 + (W_CW + k)), y[:, back:S],
                                      ALU.mult, ALU.add)
                            if k:
                                did(ins)
                            else:
                                ins.then_inc(xc_ready, 1)

            conv_loop(0, 4)
            lam = v2[:, W_LAM:W_LAM + NT]
            e_, s_, q_, p_ = (T[:, 4 * S + NT * i:4 * S + NT * (i + 1)] for i in range(4))
            did(dve.tensor_scalar(q_, lam, -1.0, None, ALU.mult))
            settle()
            dve.tensor_tensor(e_, lam, q_, ALU.max).then_inc(lam_ready, 1)
            did(dve.tensor_scalar(der[:, NT:2 * NT], v2[:, W_BR:W_BR + NT], 0.5, None, ALU.mult))
            did(dve.tensor_scalar(der[:, 2 * NT:3 * NT], v2[:, W_BI:W_BI + NT], 0.5, None, ALU.mult))
            dve.wait_ge(lam_exp, 1)
            did(dve.tensor_scalar(s_, e_, 2.0, None, ALU.add))
            settle()
            did(dve.reciprocal(s_, s_))
            settle()
            did(dve.tensor_tensor(s_, s_, e_, ALU.mult))
            settle()
            did(dve.tensor_tensor(q_, s_, s_, ALU.mult))
            settle()
            TERMS = 9
            did(dve.tensor_scalar(p_, q_, 1.0 / (2 * TERMS + 1), 1.0 / (2 * TERMS - 1), ALU.mult, ALU.add))
            settle()
            for k in range(TERMS - 2, -1, -1):
                did(dve.tensor_tensor(p_, p_, q_, ALU.mult))
                settle()
                did(dve.tensor_scalar(p_, p_, 1.0 / (2 * k + 1), None, ALU.add))
                settle()
            did(stt(p_, p_, 2.0, s_, ALU.mult, ALU.mult))
            did(dve.tensor_scalar(q_, lam, -1.0, 0.0, ALU.mult, ALU.max))
            settle()
            did(dve.tensor_tensor(p_, p_, q_, ALU.add))
            settle()
            did(dve.tensor_scalar(der[:, 0:NT], p_, -LRU_C / 2, None, ALU.mult))
            conv_loop(4, 8)

            la, ti, dk = (lambda m: tl(a2, m)), (lambda m: tl(a2, 2 + m)), (lambda m: tl(a2, 4 + m))
            for c in range(4):
                dve.wait_ge(h_out[c], DEPTH * 16 + 16)
            with chain.loop(0, GROUPS // RING, 6 * RING) as r:
                for g in range(RING):
                    y = lambda m: tl(Y, r * (2 * RING) + (2 * g + m))
                    u = RG0 + GROUP_U * g

                    def halved(m):
                        dve.wait_ge(w_used, r * (GROUP_U * RING) + (u + (3 if m == 0 else 5)))
                        stt(tl(T, m), G[m][:, :], 0.5, rs[:, :], ALU.mult, ALU.mult).then_inc(tile_out, 1)

                    def silu(m):
                        dve.wait_ge(gt_th, r * (2 * RING) + (2 * g + m + 1))
                        did(stt(tl(T, 2 + m), tl(T, 2 + m), 1.0, tl(T, m), ALU.add, ALU.mult))

                    def gate_scan(m):
                        dve.tensor_tensor(y(m), ti(m), tl(T, 2 + m), ALU.mult).then_inc(y2_ready, 1)

                    for m in range(2):
                        dve.wait_ge(xch_ready, r * (2 * RING) + (2 * g + m + 1))
                        dve.tensor_tensor(tl(XCL, m), y(m), tl(XCH, m).bitcast(F), ALU.subtract).then_inc(xcl_ready, 1)
                    dve.wait_ge(ri_taken, r * (4 * RING) + (4 * g + 4))
                    for m in range(2):
                        dve.tensor_scalar(la(m), la(m), 1.0, col(der, r * (2 * RING) + (2 * g + m)), ALU.add,
                                          ALU.mult).then_inc(la_ready, 1)
                    for m in range(2):
                        stt(y(m), ti(m), 1.0, y(m), ALU.add, ALU.mult).then_inc(la_ready, 1)
                    halved(0)
                    dve.wait_ge(lru_exp, r * (6 * RING) + (6 * g + 6))
                    for m in range(2):
                        stt(la(m), ti(m), 1.0, la(m), ALU.add, ALU.mult).then_inc(var_ready, 1)
                    silu(0)
                    dve.wait_ge(la_ready, r * (4 * RING) + (4 * g + 4))
                    dve.wait_ge(lru_root, r * (2 * RING) + (2 * g + 2))
                    for m in range(2):
                        did(stt(y(m), la(m), 0.5, y(m), ALU.mult, ALU.mult))
                    for m in range(2):
                        settle(1)
                        did(dve.tensor_tensor_scan(ti(m), dk(m), y(m), 0.0, ALU.mult, ALU.add))
                    settle()
                    gate_scan(0)
                    halved(1)
                    silu(1)
                    settle()
                    gate_scan(1)
            for t in range(NT):
                xlow(t, tl(Y, t), xb + NT + t + 1)

            did(dve.memset(acc[:, :], 0.0))
            settle()

            def oloop(lo, hi):
                with chain.loop(lo, hi, 2) as i:
                    for j in range(2):
                        t = i * 2 + j
                        for c in range(4):
                            dve.wait_ge(h_in[c], DEPTH * 16 + 32)
                        did(stt(tl(H, t), tl(H, t), col(v2, t + W_FG), rs1, ALU.mult, ALU.mult))
                        dve.wait_ge(osq_ready, t + 1)
                        dve.tensor_tensor(acc[:, :], acc[:, :], tl(T, j), ALU.add).then_inc(osum_ready, 1)
                        dve.tensor_scalar(tl(Y, t), G[j][:, :], col(v2, t + W_POST), None, ALU.mult).then_inc(tile_out, 1)
                        dve.wait_ge(osum_ready, t + 1)

            oloop(0, 4)
            dve.wait_ge(ph_ready, DEPTH + 1)
            dve.tensor_tensor(PL[:, :], praw, PH[:, :].bitcast(F), ALU.subtract).then_inc(pl_ready, 1)
            oloop(4, 8)

            dve.wait_ge(root_ready, DEPTH * 3 + 3)
            dve.reciprocal(rs[:, :], rs[:, :]).then_inc(ors_ready, 1)
            dve.wait_ge(ors_ready, 1)
            settle()
            LAG = 6
            for t in range(NT + LAG):
                if t < NT:
                    if t % 2 == 0:
                        did(dve.tensor_tensor(tl(Y, t), tl(Y, t), rs[:, :], ALU.mult))
                        settle()
                    else:
                        dve.wait_ge(o_scaled, t // 2 + 1)
                    dve.tensor_tensor(tl(H, t), tl(H, t), tl(Y, t), ALU.add).then_inc(h2_ready, 1)
                if t >= LAG:
                    xlow(t - LAG, tl(H, t - LAG), xb + 2 * NT + t - LAG + 1)

            dve.wait_ge(h2_ready, NT)

            def wloop(lo, hi, e):
                with chain.loop(lo, hi, 2) as i:
                    for j in range(2):
                        t = i * 2 + j
                        dve.wait_ge(w_used, i * 4 + (WG0 + 2 * j + 2))
                        dve.tensor_scalar(tl(T, j), G[j][:, :], 0.5, None, ALU.mult).then_inc(tile_out, 1)
                        dve.wait_ge(wg_th, t + 1)
                        did(stt(tl(T, j), tl(T, j), 1.0, e(t), ALU.add, ALU.mult))
                        settle()
                        dve.tensor_tensor(tl(H, t), tl(H, t), tl(T, j), ALU.add).then_inc(o_ready, 1)

            dve.wait_ge(e_out, DEPTH * NT + 4)
            wloop(0, 2, lambda t: tl(T, t + 2))
            dve.wait_ge(e_out, DEPTH * NT + NT)
            wloop(2, 8, lambda t: tl(Y, t - 4))

        @block.tensor
        def _(pe):
            def three(bank, s, wt, xh, xl, first, last):
                c = slice(s * UW + wt * P, s * UW + (wt + 1) * P)
                pe.matmul(bank, WH[:, c], xh, start=first, stop=False)
                pe.matmul(bank, WH[:, c], xl, start=False, stop=False)
                return pe.matmul(bank, WL[:, c], xh, start=False, stop=last)

            def unit(u, s, half, bank, x_first=None):
                pe.wait_ge(wl_ready, u + 1)
                for k in range(UT):
                    kt = half * UT + k
                    if x_first is not None:
                        pe.wait_ge(xl_ready, x_first + (kt + 1))
                    last = three(bank[:, :], s, k, tl(XH, kt), tl(XL, kt), kt == 0, kt == NT - 1)
                last.then_inc(w_used, 1)

            def tile(n, u, s, bank, x_first=None):
                pe.wait_ge(tile_out, n + 1)
                unit(u, s, 0, bank, x_first)
                unit(u + 1, s + 1, 1, bank, x_first)

            def two_tiles(n, u, x_first):
                tile(n, u, 0, G[0], x_first)
                tile(n + 1, u + 2, 2, G[1])

            def tiles(n, u, x_first, count, lo=0):
                with pe.Fori(lo, count // 2) as i:
                    two_tiles(n + i * 2, u + i * 4, x_first)

            def stat():
                pe.matmul(N[:, :], ones[:, :], acc[:, :], start=True, stop=True).then_inc(stat_done, 1)

            pe.wait_ge(relb_in, 48)
            pe.matmul(SC[0][0:HQ, :], ones[0:32, 0:HQ], T[0:32, 0:S], start=True, stop=True).then_inc(line_mm, 1)
            pe.wait_ge(ident_in, 16)

            def embed(first, n, sums):
                for t in range(NT):
                    j, c = t // 4, t % 4
                    if c == 0:
                        pe.wait_ge(wl_ready, first + (j + 1))
                    if t >= 4:
                        pe.wait_ge(e_out, n * NT + (t - 3))
                    for k in range(PK):
                        last = three(FOUR[c][:, :], j, PK * c + k, tl(PH, k), tl(PL, k), k == 0, k == PK - 1)
                    last.then_inc(e_done if c < 3 else w_used, 1)
                    if t == 1 and sums is not None:
                        pe.wait_ge(osum_ready, sums)
                        stat()

            with pe.Fori(0, DEPTH) as ly:
                u0 = ly * LAYER_U
                n0 = ly * LAYER_N
                x0 = ly * (3 * NT)

                for k in range(6):
                    pe.wait_ge(tile_out, n0 + (k + 1))
                    unit(u0 + 2 * k, 2 * k % RING, 0, G[k % 2], x0 if k == 0 else None)
                    if k == 1:
                        pe.wait_ge(ones_ready, 1)
                        pe.wait_ge(hsum_ready, ly * NT + NT)
                        stat()
                    unit(u0 + (2 * k + 1), (2 * k + 1) % RING, 1, G[k % 2], x0 if k == 0 else None)
                with pe.Fori(1, CT // 2) as i:
                    for k in range(6):
                        tile(n0 + (i * 6 + k), u0 + (i * 12 + 2 * k), 2 * k % RING, G[k % 2])
                for k in range(4):
                    u = u0 + (KV0 + 2 * k)
                    pe.wait_ge(tile_out, n0 + (N_KV + k + 1))
                    unit(u, 2 * k % RING, 0, G[k % 2])
                    if k == 3:
                        pe.wait_ge(vsum_ready, ly * CT + CT)
                        stat()
                    unit(u + 1, (2 * k + 1) % RING, 1, G[k % 2])
                    if k == 1:
                        pe.wait_ge(ysum_ready, ly * CT + CT)
                        stat()
                pe.wait_ge(tile_out, n0 + (N_Z + 2))
                for j in range(2):
                    for t in range(NB):
                        c = slice(t * P, (t + 1) * P)
                        last = pe.transpose(TR[j][:, c], tl(H, PT + j)[:, c], ident[:, :])
                    last.then_inc(vtr_done, 1)

                def scores(n):
                    t, b, kt, lo, nk = pair_of(n)
                    if n:
                        pe.wait_ge(scores_taken, ly * (2 * PAIRS) + 2 * n)
                    for hh in range(2):
                        r = slice(hh * DH, (hh + 1) * DH)
                        pe.matmul(SC[hh][:, 0:nk * BLK], tl(H, QT + t)[r, b * BLK:(b + 1) * BLK],
                                  tl(H, KT + kt)[r, lo * BLK:(lo + nk) * BLK],
                                  start=True, stop=True).then_inc(scores_done, 1)

                def turn(n):
                    nk = pair_of(n)[4]
                    pe.wait_ge(probs_ready, ly * (2 * PAIRS) + (2 * n + 2))
                    if n == 0:
                        pe.wait_ge(v_ready, ly * 2 + 2)
                    else:
                        pe.wait_ge(pt_ready, ly * (2 * PAIRS) + 2 * n)
                    for hh in range(2):
                        for k in range(nk):
                            c = slice(k * BLK, (k + 1) * BLK)
                            last = pe.transpose(TR[hh][:, c], pbuf(n)[:, (3 * hh + k) * BLK:(3 * hh + k + 1) * BLK], ident[:, :])
                        last.then_inc(tr_done, 1)

                def values(n):
                    _, _, kt, lo, nk = pair_of(n)
                    pe.wait_ge(pt_ready, ly * (2 * PAIRS) + (2 * n + 2))
                    if n:
                        pe.wait_ge(att_ready, ly * PAIRS + n)
                    for k in range(nk):
                        for hh in range(2):
                            v0 = VT * S + (lo + k) * 2 * P + (2 * kt + hh) * DH
                            last = pe.matmul(VB[hh * DH:(hh + 1) * DH, 0:BLK], H[:, v0:v0 + DH],
                                             H[:, PT * S + (2 * k + hh) * BLK:PT * S + (2 * k + hh + 1) * BLK],
                                             start=(k == 0), stop=(k == nk - 1))
                    last.then_inc(pv_done, 1)

                for n, u in enumerate(UNIT_AT):
                    for kt in range(Z_CUTS[n], Z_CUTS[n + 1]):
                        v, k = kt // UT, kt % UT
                        if kt % NT == 0:
                            pe.wait_ge(tile_out, n0 + (N_Z + kt // NT + 1))
                        if k == 0:
                            pe.wait_ge(wl_ready, u0 + (Z0 + v + 1))
                        last = three(G[kt // NT % 2][:, :], v % RING, k, tl(XH, kt % NT), tl(XL, kt % NT),
                                     kt % NT == 0, kt % NT == NT - 1)
                        if k == UT - 1:
                            last.then_inc(w_used, 1)
                    if n < PAIRS:
                        scores(n)
                    if 3 <= n < PAIRS + 3:
                        values(n - 3)
                    if 2 <= n < PAIRS + 2:
                        turn(n - 2)

                tiles(n0 + N_OUT, u0 + OUT0, x0 + NT, NT)

                pe.wait_ge(pl_ready, ly + 1)
                embed(u0 + PE0, ly, None)
                two_tiles(n0 + N_PG, u0 + PG0, x0 + 2 * NT)
                pe.wait_ge(esum_ready, ly * NT + NT)
                stat()
                tiles(n0 + N_PG, u0 + PG0, x0 + 2 * NT, NT, 1)

            xb = DEPTH * 3 * NT
            tile(NB0, XB0, 0, G[0], xb)
            pe.wait_ge(hsum_ready, DEPTH * NT + NT)
            stat()
            pe.wait_ge(fsum_ready, DEPTH * (NT + 1))
            pe.matmul(VB[:, :], ones[:, :], tl(T, 4), start=True, stop=True).then_inc(stat_done, 1)
            tile(NB0 + 1, XB0 + 2, 2, G[1])
            tiles(NB0, XB0, xb, NT, 1)
            with pe.Fori(0, GROUPS // RING) as r:
                for g in range(RING):
                    k = GROUP_U * g
                    n = r * (2 * RING) + (NB0 + 16 + 2 * g)
                    u = r * (GROUP_U * RING) + (RG0 + k)

                    for j in range(GROUP_U):
                        s = (k + j) % RING
                        if j == 1:
                            pe.wait_ge(wl_ready, u + 2)
                            pe.wait_ge(xcl_ready, r * (2 * RING) + (2 * g + 2))
                            for c in range(4):
                                for q in range(2):
                                    last = three(FOUR[c][:, :], s, 2 * c + q, tl(XCH, q), tl(XCL, q), q == 0, q == 1)
                            last.then_inc(w_used, 1)
                        else:
                            m, h = ((0, 0), None, (0, 1), (1, 0), (1, 1))[j]
                            if h == 0:
                                pe.wait_ge(tile_out, n + (m + 1))
                            unit(u + j, s, h, G[m])
            tiles(NB0 + 32, WO0, xb + NT, NT)
            pe.wait_ge(pl_ready, DEPTH + 1)
            embed(WP0, DEPTH, NT)
            tiles(NB0 + 48, WG0, xb + 2 * NT, NT)


def units_of(a):
    k, n = a.shape
    return a.reshape(k // P, P, n // P, P).transpose(2, 1, 0, 3).reshape(n // P, P, 2, UW).transpose(0, 2, 1, 3).reshape(-1, P, UW)


def embed_units(a):
    return a.reshape(PK, P, 4, 4, P).transpose(2, 1, 3, 0, 4).reshape(4, P, UW)


def gate_units(r, i):
    import numpy as np
    both = np.stack([r, i], 1)
    return both.reshape(8, 2, 2, P, 2, P).transpose(0, 3, 1, 4, 2, 5).reshape(8, P, UW)


def heads(a, axis):
    import numpy as np
    shape = list(a.shape)
    b = np.moveaxis(a, axis, 0).reshape(2, 2, GQ, DH, -1).swapaxes(1, 2).reshape(shape[axis], -1)
    return np.moveaxis(b.reshape([shape[axis]] + shape[:axis] + shape[axis + 1:]), 0, axis)


def pairs(a):
    return a.reshape(*a.shape[:-1], 2, 2, GQ).swapaxes(-1, -2).reshape(a.shape)


def columns(a):
    return a.reshape(-1, P).T


def wide(a):
    return a.T.reshape(-1, P, a.shape[0]).transpose(1, 0, 2).reshape(P, -1)


def distance_tables():
    import numpy as np
    buckets, far = 32, 128
    rel = np.arange(-2 * BLK + 1, 2 * BLK)
    half = buckets // 2
    n = np.abs(rel)
    exact = half // 2
    large = exact + (np.log(np.maximum(n, 1) / exact) / np.log(far / exact) * (half - exact)).astype(np.int32)
    bucket = (rel > 0) * half + np.where(n < exact, n, np.minimum(large, half - 1))
    inside = n <= BLK
    onehot = np.zeros((buckets, S), np.float32)
    onehot[bucket[inside], np.nonzero(inside)[0]] = 1.0
    band = np.full((HQ, S), NEG, np.float32)
    band[:, np.nonzero(inside)[0]] = 0.0
    return onehot, band


def kernel(**inputs):
    import numpy as np
    import concourse.bacc as bacc
    from concourse.bass_utils import run_bass_kernel_spmd as run

    a = {k: np.asarray(v) for k, v in inputs.items()}
    stream, vectors = [], []
    for l in range(DEPTH):
        wi = a["w_in"][l]
        val, glu, az, q, k, v, bz = np.split(wi, np.cumsum([WC, WC, WC, WC, HKV * DH, HKV * DH]), axis=1)
        q, bz = heads(q, 1), heads(bz, 1)
        inter = np.stack([m.reshape(D, CT, P) for m in (glu, val, q)], 2).reshape(D, -1)
        stream.append(units_of(np.concatenate([inter, k, v, az, bz], 1)))
        wo = a["w_out"][l]
        stream.append(units_of(np.concatenate([wo[:WC], heads(wo[WC:], 0)], 0)))
        stream.append(embed_units(a["w_pe"][l]))
        stream.append(units_of(a["w_pg"][l]))
        vectors.append(np.concatenate(
            [columns(a["pe_g"][l]), columns(a["conv_b"][l]), columns(a["cln_g"][l]),
             columns(a["cln_b"][l]), np.broadcast_to(pairs(a["sink"][l]), (P, HQ)),
             a["conv_w"][l].T.reshape(CT, P, TAPS).transpose(1, 0, 2).reshape(P, -1)], 1))
    conv_half, gate_half = np.split(units_of(a["a_w_in_2"][0]), 2)
    gate_half = gate_half.reshape(GROUPS, GROUP_U - 1, P, UW)
    gates = gate_units(a["a_w_r_2"][0], a["a_w_i_2"][0])[:, None]
    stream.append(conv_half)
    stream.append(np.concatenate([gate_half[:, :1], gates, gate_half[:, 1:]], 1).reshape(-1, P, UW))
    stream.append(units_of(a["a_w_out_2"][0]))
    stream.append(embed_units(a["ple_w_proj_2"][0]))
    stream.append(units_of(a["ple_w_gate_2"][0]))
    vec2 = np.concatenate(
        [columns(a[n].reshape(-1)) for n in ("final_g", "norm_pre_2", "norm_post_2", "a_conv_b_2", "a_b_r_2",
                                             "a_b_i_2", "a_lam_2")]
        + [a["a_conv_w_2"][0].T.reshape(NT, P, TAPS2).transpose(1, 0, 2).reshape(P, -1),
           *(columns(g) for g in a["norm_g"]), columns(a["final_g"])], 1)
    onehot, band = distance_tables()
    arrays = {
        "x": wide(a["x"][0]),
        "pin": np.stack([wide(a["p"][0, 0]), wide(a["p"][1, 0]), wide(a["p_2"][0, 0])]),
        "lvec": np.stack(vectors), "vec2": vec2, "relb": pairs(a["rel_bias"]), "onehot": onehot, "band": band,
        "ident": np.eye(P, dtype=np.float32), "w": np.concatenate(stream, 0),
    }
    arrays = {k: np.ascontiguousarray(v, np.float32) for k, v in arrays.items()}

    nc = bacc.Bacc("TRN2", target_bir_lowering=False, num_devices=1)
    args = [nc.dram_tensor(f"in_{k}", v.shape, mybir.dt.float32, kind="ExternalInput").ap() for k, v in arrays.items()]
    out = nc.dram_tensor("out", (P, NT * S), mybir.dt.float32, kind="ExternalOutput").ap()
    build(nc, *args, out)
    r = run(nc, [{f"in_{k}": v for k, v in arrays.items()}], core_ids=[0])
    y = r.results[0]["out"]
    return y.reshape(P, NT, S).transpose(1, 0, 2).reshape(D, S).T.reshape(1, S, D)
```
